# Optimizing a Trainium2 kernel written in Bass

```python
import math
import jax, jax.numpy as jnp
from jax import lax
import numpy as np

D_MODEL = 1024
BATCH = 1
SEQ = 512
DEPTH = 1

CHUNK = 64
HEAD_DIM = 64
A_HEADS = 8
A_LEFT_CHUNKS = 8
A_BAND = (A_LEFT_CHUNKS + 1) * CHUNK
A_MAX_REL = 128
B_Q_HEADS = 8
B_KV_HEADS = 2
B_GROUP = B_Q_HEADS // B_KV_HEADS
B_WINDOW = 128
B_BAND_CHUNKS = B_WINDOW // CHUNK
B_BAND = B_BAND_CHUNKS * CHUNK
D_A = A_HEADS * HEAD_DIM
D_BQ = B_Q_HEADS * HEAD_DIM
D_BKV = B_KV_HEADS * HEAD_DIM
N_BRANCH = 2
D_IN = 3 * D_A + D_BQ + 2 * D_BKV + N_BRANCH * D_MODEL
D_FF = ((8 * D_MODEL // 3 + 255) // 256) * 256
ROPE_THETA = 10000.0
RMS_EPS = 1e-6
FFN_RES = 0.5
NEG_INF = -1e30

kernel_name = "hybrid_chunked_relbias_swa_sink_macaron"

def rmsnorm(x, g):
    xf = x.astype(jnp.float32)
    y = xf * lax.rsqrt(jnp.mean(xf * xf, axis=-1, keepdims=True) + RMS_EPS)
    return (y * g.astype(jnp.float32)).astype(x.dtype)

def swiglu(x, w_gu, w_down):
    g, u = jnp.split(x @ w_gu, 2, axis=-1)
    return (jax.nn.silu(g) * u) @ w_down

def rope(x, positions):
    half = HEAD_DIM // 2
    inv_freq = ROPE_THETA ** (-jnp.arange(half, dtype=jnp.float32) / half)
    ang = positions.astype(jnp.float32)[:, None] * inv_freq[None, :]
    cos = jnp.cos(ang)[None, :, None, :]
    sin = jnp.sin(ang)[None, :, None, :]
    xf = x.astype(jnp.float32)
    x1, x2 = xf[..., :half], xf[..., half:]
    out = jnp.concatenate([x1 * cos - x2 * sin, x2 * cos + x1 * sin], axis=-1)
    return out.astype(x.dtype)

def chunked_relbias_attention(q, k, v, rel_bias):
    b, s, h, dh = q.shape
    nc = s // CHUNK
    pad = A_LEFT_CHUNKS * CHUNK
    kp = jnp.pad(k, ((0, 0), (pad, 0), (0, 0), (0, 0)))
    vp = jnp.pad(v, ((0, 0), (pad, 0), (0, 0), (0, 0)))
    q_loc = jnp.arange(CHUNK)
    k_loc = jnp.arange(A_BAND)
    dist = q_loc[:, None] + pad - k_loc[None, :]
    idx = jnp.clip(dist, -A_MAX_REL, A_MAX_REL) + A_MAX_REL
    bias = rel_bias.astype(jnp.float32)[:, idx]
    scale = HEAD_DIM ** -0.5
    qc = jnp.moveaxis(q.reshape(b, nc, CHUNK, h, dh), 1, 0)

    def one_chunk(args):
        c, q_blk = args
        start = c * CHUNK
        k_band = lax.dynamic_slice_in_dim(kp, start, A_BAND, axis=1)
        v_band = lax.dynamic_slice_in_dim(vp, start, A_BAND, axis=1)
        sc = jnp.einsum('bqhd,bkhd->bhqk', q_blk, k_band).astype(jnp.float32) * scale + bias[None]
        valid = (start + k_loc) >= pad
        sc = jnp.where(valid[None, None, None, :], sc, NEG_INF)
        p = jax.nn.softmax(sc, axis=-1).astype(v.dtype)
        return jnp.einsum('bhqk,bkhd->bqhd', p, v_band)

    out = lax.map(one_chunk, (jnp.arange(nc), qc))
    return jnp.moveaxis(out, 0, 1).reshape(b, s, h * dh)

def sliding_window_sink_gqa(q, k, v, sinks):
    b, s, hq, dh = q.shape
    nc = s // CHUNK
    qc = q.reshape(b, nc, CHUNK, B_KV_HEADS, B_GROUP, dh)
    kc = k.reshape(b, nc, CHUNK, B_KV_HEADS, dh)
    vc = v.reshape(b, nc, CHUNK, B_KV_HEADS, dh)

    def band(t):
        tp = jnp.pad(t, ((0, 0), (B_BAND_CHUNKS - 1, 0), (0, 0), (0, 0), (0, 0)))
        return jnp.concatenate([tp[:, i:i + nc] for i in range(B_BAND_CHUNKS)], axis=2)

    k_band = band(kc)
    v_band = band(vc)
    key_chunk = (jnp.arange(nc)[:, None] - (B_BAND_CHUNKS - 1)
                 + jnp.arange(B_BAND)[None, :] // CHUNK)
    valid = key_chunk >= 0
    scale = HEAD_DIM ** -0.5
    sc = jnp.einsum('bcqgjd,bckgd->bcgjqk', qc, k_band).astype(jnp.float32) * scale
    sc = jnp.where(valid[None, :, None, None, None, :], sc, NEG_INF)
    sink = sinks.astype(jnp.float32).reshape(B_KV_HEADS, B_GROUP)[None, None, :, :, None, None]
    m = jnp.maximum(jnp.max(sc, axis=-1, keepdims=True), sink)
    e = jnp.exp(sc - m)
    p = (e / (jnp.sum(e, axis=-1, keepdims=True) + jnp.exp(sink - m))).astype(v.dtype)
    out = jnp.einsum('bcgjqk,bckgd->bcqgjd', p, v_band)
    return out.reshape(b, s, hq * dh)

def setup_inputs(seed: int = 0) -> dict:
    key = jax.random.key(seed)
    ks = jax.random.split(key, 16)
    f32 = jnp.float32

    def w(k, shape, fan_in):
        return jax.random.normal(k, shape, f32) * (fan_in ** -0.5)

    def gain(k):
        return 1.0 + 0.02 * jax.random.normal(k, (DEPTH, D_MODEL), f32)

    return {
        "x": jax.random.normal(ks[0], (BATCH, SEQ, D_MODEL), f32),
        "g_ffn1": gain(ks[1]),
        "w_ffn1_gu": w(ks[2], (DEPTH, D_MODEL, 2 * D_FF), D_MODEL),
        "w_ffn1_down": w(ks[3], (DEPTH, D_FF, D_MODEL), D_FF),
        "g_mix": gain(ks[4]),
        "w_in": w(ks[5], (DEPTH, D_MODEL, D_IN), D_MODEL),
        "a_rel_bias": 0.5 * jax.random.normal(ks[6], (DEPTH, A_HEADS, 2 * A_MAX_REL + 1), f32),
        "b_sinks": jax.random.normal(ks[7], (DEPTH, B_Q_HEADS), f32),
        "w_branch_a": w(ks[8], (DEPTH, D_A, D_MODEL), D_A),
        "w_branch_b": w(ks[9], (DEPTH, D_BQ, D_MODEL), D_BQ),
        "w_out": w(ks[10], (DEPTH, D_MODEL, D_MODEL), D_MODEL),
        "g_ffn2": gain(ks[11]),
        "w_ffn2_gu": w(ks[12], (DEPTH, D_MODEL, 2 * D_FF), D_MODEL),
        "w_ffn2_down": w(ks[13], (DEPTH, D_FF, D_MODEL), D_FF),
        "g_final": 1.0 + 0.02 * jax.random.normal(ks[14], (D_MODEL,), f32),
    }

def reference(x, g_ffn1, w_ffn1_gu, w_ffn1_down, g_mix, w_in, a_rel_bias, b_sinks,
              w_branch_a, w_branch_b, w_out, g_ffn2, w_ffn2_gu, w_ffn2_down, g_final):
    b, s, _ = x.shape
    positions = jnp.arange(s)
    split_at = np.cumsum([D_A, D_A, D_A, D_BQ, D_BKV, D_BKV, D_MODEL]).tolist()
    h = x
    for l in range(DEPTH):
        h = h + FFN_RES * swiglu(rmsnorm(h, g_ffn1[l]), w_ffn1_gu[l], w_ffn1_down[l])

        u = rmsnorm(h, g_mix[l])
        qa, ka, va, qb, kb, vb, gate_a, gate_b = jnp.split(u @ w_in[l], split_at, axis=-1)
        qa = qa.reshape(b, s, A_HEADS, HEAD_DIM)
        ka = ka.reshape(b, s, A_HEADS, HEAD_DIM)
        va = va.reshape(b, s, A_HEADS, HEAD_DIM)
        qb = rope(qb.reshape(b, s, B_Q_HEADS, HEAD_DIM), positions)
        kb = rope(kb.reshape(b, s, B_KV_HEADS, HEAD_DIM), positions)
        vb = vb.reshape(b, s, B_KV_HEADS, HEAD_DIM)

        y_a = chunked_relbias_attention(qa, ka, va, a_rel_bias[l]) @ w_branch_a[l]
        y_b = sliding_window_sink_gqa(qb, kb, vb, b_sinks[l]) @ w_branch_b[l]
        merged = jax.nn.sigmoid(gate_a) * y_a + jax.nn.sigmoid(gate_b) * y_b
        h = h + merged @ w_out[l]

        h = h + FFN_RES * swiglu(rmsnorm(h, g_ffn2[l]), w_ffn2_gu[l], w_ffn2_down[l])
    return rmsnorm(h, g_final)


_drawn_inputs = setup_inputs


def setup_inputs(seed=0):
    import zlib

    import numpy as np

    out = dict(_drawn_inputs(seed))
    spreads = {}
    factors = {'g_ffn1': 6.101, 'g_mix': 8.0, 'b_sinks': 8.0, 'g_ffn2': 7.181, 'g_final': 2.873}
    for name, (base, spread) in spreads.items():
        noise = np.random.default_rng([zlib.crc32(name.encode()), seed]).standard_normal(out[name].shape)
        drawn = base * np.exp(spread * noise) if base else spread * noise
        out[name] = __import__('jax').numpy.asarray(drawn.astype(out[name].dtype))
    for name, factor in factors.items():
        out[name] = (out[name] * factor).astype(out[name].dtype)
    return out
```

```python
from contextlib import ExitStack

import concourse.bass as bass
from concourse import mybir

ALU = mybir.AluOpType
ACT = mybir.ActivationFunctionType
F32 = mybir.dt.float32
F32R = mybir.dt.float32r

P = 128
D = 1024
S = 512
FF = 2816
DK = D // P
FK = FF // P
QT = S // P
CH = 64
HD = 64
HEADS = 8
D_ATT = HEADS * HD
MAX_REL = 128
EPS = 1e-6
SCALE = HD ** -0.5
MASKED = -1e30 / SCALE
CW = 256
GU = FF // CW
DOWN_KB = (6, 5, 6, 5)
DOWN_K0 = (0, 6, 11, 17)
NPAIR = D // CW
EXT = S + P
PRODUCTS = ((0, 0), (0, 1), (1, 0))

QA0, KA0, VA0, QB0 = 0, D_ATT, 2 * D_ATT, 3 * D_ATT
KVB0 = 4 * D_ATT
GA0 = KVB0 + 4 * HD
GB0 = GA0 + D

FFN_CHUNKS = 2 * GU + NPAIR * len(DOWN_KB)
C_MIX = FFN_CHUNKS

MIX = [("qa", 0, DK), ("ka", 0, DK), ("va", 0, DK),
       ("qa", 1, DK), ("ka", 1, DK), ("va", 1, DK),
       ("qb", 0, DK), ("qb", 1, DK), ("kvb", 0, DK)]
for _c in range(NPAIR):
    MIX += [("ga", _c, DK), ("ya", _c, DK // 2)]
for _c in range(NPAIR):
    MIX += [("gb", _c, DK), ("yb", _c, DK // 2)]
N_TILED = len(MIX)
MIX += [("out", _c, DK) for _c in range(NPAIR)]
C_OUT = C_MIX + N_TILED
C_FFN2 = C_MIX + len(MIX)
N_CHUNKS = C_FFN2 + FFN_CHUNKS

BEFORE = [(c, m) for c in range(3) for m in range(2)]
FILL = [[(3, 0), (3, 1)], [(4, 0), (4, 1)], [(5, 0), (5, 1)], [(6, 0), (6, 1)],
        [(7, 0)], [(7, 1)], [(8, 0)], [(8, 1)]]
for _c in range(NPAIR):
    FILL += [[(9 + 2 * _c, 0), (9 + 2 * _c, 1)], [(10 + 2 * _c, 0), (10 + 2 * _c, 1)]]
AFTER = [(c, m) for c in range(17, N_TILED) for m in range(2)]
TILES = BEFORE + [x for f in FILL for x in f] + AFTER
NH = 2 * HEADS


def kb_of(c):
    if C_MIX <= c < C_FFN2:
        return MIX[c - C_MIX][2]
    d = c if c < C_MIX else c - C_FFN2
    return DK if d < 2 * GU else DOWN_KB[(d - 2 * GU) % len(DOWN_KB)]


def tile_kind(tau):
    c, m = TILES[tau]
    kind, i, _ = MIX[c]
    if kind == "kvb":
        kind = ("kb", "vb")[m]
    return kind, i, m


ROPED = [t for t in range(len(TILES)) if tile_kind(t)[0] in ("qb", "kb")]
GATES = [t for t in range(len(TILES)) if tile_kind(t)[0] in ("ga", "gb")]
SPLIT = [t for t in range(len(TILES)) if tile_kind(t)[0] not in ("ga", "gb", "ya")]
MERGED = [t for t in range(len(TILES)) if tile_kind(t)[0] == "yb"]


def loaded_at(c):
    qb = C_MIX + MIX.index(("qb", 0, DK))
    return 32 * (c // 2 + 1) + (32 if c >= qb else 0)


def used_at(c):
    return c + 1 if c < C_MIX else None if c < C_OUT else c + 1 - N_TILED


def n_keys(s, i):
    first = 0 if s < HEADS else max(0, i - 1) * P
    return first, (i + 1) * P - first


def build(nc, x, g_ffn1, w_ffn1_gu, w_ffn1_down, g_mix, w_in, a_rel_bias, b_sinks, w_branch_a,
          w_branch_b, w_out, g_ffn2, w_ffn2_gu, w_ffn2_down, g_final, identity, rope, out):
    ext_dram = nc.dram_tensor("rel_bias_ext", (HEADS, EXT), F32, kind="Internal")

    ctx = ExitStack()

    def sb(stack, name, shape, dt=F32):
        return stack.enter_context(nc.sbuf_tensor(name, shape, dt))

    def psum(name, shape):
        return ctx.enter_context(nc.psum_tensor(name, shape, F32))

    def sem(name):
        return ctx.enter_context(nc.semaphore(name))

    with ctx:
        raw = sb(ctx, "raw", [P, 2, DK, CW])
        w_hl = sb(ctx, "w_hl", [P, 2, 2, DK, CW], F32R)
        xn = sb(ctx, "xn", [P, 2, DK, S], F32R)
        h = sb(ctx, "h", [P, DK, S])
        ident = sb(ctx, "ident", [P, P])
        ones = sb(ctx, "ones", [P, P])
        gains = sb(ctx, "gains", [P, 3, DK])
        eps = sb(ctx, "eps", [P, 1])
        stat = sb(ctx, "stat", [P, 8])
        rows = sb(ctx, "rows", [P, 4])
        norm_s = sb(ctx, "norm_s", [P, 2, S])
        sinks = sb(ctx, "sinks", [P, HEADS])
        relrow = sb(ctx, "relrow", [HEADS, 2 * MAX_REL + 1])

        ffn = ExitStack()
        hid = sb(ffn, "hid", [P, 2, FK, S], F32R)
        silu = sb(ffn, "silu", [P, 2, S])
        work = sb(ffn, "work", [P, 2, S])
        ffn.close()
        ends = ExitStack()
        xin = sb(ends, "xin", [P, QT, D])
        xs = sb(ends, "xs", [P, QT, D])
        g_fin = sb(ends, "g_fin", [P, D])
        junk = sb(ends, "junk", [P, D])
        extrow = sb(ends, "extrow", [HEADS, EXT])
        ends.close()
        att = ExitStack()
        qa = sb(att, "qa", [P, 4, 2, S], F32R)
        qb = sb(att, "qb", [P, 4, 2, S], F32R)
        kk = sb(att, "kk", [P, 4, 2, S], F32R)
        vv = sb(att, "vv", [P, 4, 2, QT, 3, HD], F32R)
        pt = sb(att, "pt", [P, 2, QT, S], F32R)
        sc = sb(att, "sc", [P, 10 * P])
        bias_a = sb(att, "bias_a", [P, 2, S])
        mask_b = sb(att, "mask_b", [P, 2 * P])
        cs = sb(att, "cs", [P, 2, S])
        att.close()
        over = ExitStack()
        sb(over, "over_pad", [P, (3 * 8 * S + 2 * QT * 3 * HD)])
        y_gated = sb(over, "y_gated", [P, DK, S])
        over.close()
        roped = norm_s

        pj = psum("pj", [P, 4, S])
        ps = psum("ps", [P, 2, S])
        po = psum("po", [P, 2, S])

        raw_in = [sem("raw_in0"), sem("raw_in1")]
        hi_done = sem("hi_done")
        lo_done = sem("lo_done")
        used = sem("used")
        consts_in = sem("consts_in")
        x_in = [sem(f"x_in{i}") for i in range(QT)]
        fin_in = sem("fin_in")
        ones_set = sem("ones_set")
        zeros_set = sem("zeros_set")
        dve = sem("dve")
        actc = sem("actc")
        pool = sem("pool")
        sq_done = sem("sq_done")
        rms_done = sem("rms_done")
        xs_done = sem("xs_done")
        xt_done = sem("xt_done")
        xt_hi = sem("xt_hi")
        xt_lo = sem("xt_lo")
        ht_done = sem("ht_done")
        ht_used = sem("ht_used")
        silu_done = sem("silu_done")
        gated = sem("gated")
        hid_hi = sem("hid_hi")
        hid_lo = sem("hid_lo")
        h_done = sem("h_done")
        sq_pair = sem("sq_pair")
        acc_done = sem("acc_done")
        ms_done = sem("ms_done")
        rms_sqrt = sem("rms_sqrt")
        norm_t = sem("norm_t")
        norm_hi = sem("norm_hi")
        norm_lo = sem("norm_lo")
        ext_set = sem("ext_set")
        ext_out = sem("ext_out")
        bias_in = sem("bias_in")
        bias_ready = sem("bias_ready")
        tile_done = sem("tile_done")
        tile_free = [sem("tile_free0"), sem("tile_free1")]
        rope_sum = sem("rope_sum")
        split_hi = sem("split_hi")
        roped_lo = sem("roped_lo")
        merged_lo = sem("merged_lo")
        gate_exp = sem("gate_exp")
        merged_sum = sem("merged_sum")
        s_done = sem("s_done")
        s_used = sem("s_used")
        neg_done = sem("neg_done")
        exp_done = sem("exp_done")
        p_done = sem("p_done")
        t_done = sem("t_done")
        pt_hi = sem("pt_hi")
        pt_lo = sem("pt_lo")
        pv_done = sem("pv_done")
        o_hi = sem("o_hi")
        o_lo = sem("o_lo")
        yt_done = sem("yt_done")
        yt_used = sem("yt_used")
        y_done = sem("y_done")
        out_done = sem("out_done")

        def f32(ap):
            return ap.bitcast(F32)

        def wait_used(eng, c):
            if C_MIX <= c < C_OUT:
                eng.wait_ge(tile_done, 2 * (c - C_MIX + 1))
            else:
                eng.wait_ge(used, used_at(c))

        block = ctx.enter_context(nc.Block())

        @block.sync
        def _(sp):
            def load(c, slot, halves):
                if not isinstance(c, int) or c >= 2:
                    sp.wait_ge(lo_done, c - 1)
                for dst, src in halves:
                    sp.dma_start(dst, src).then_inc(raw_in[slot], 16)

            def by_rows(slot, src, kb):
                k = kb // 2
                return [(raw[:, slot, 0:k, :], src[:, 0:k, :]), (raw[:, slot, k:kb, :], src[:, k:kb, :])]

            def load_ffn(c0, w_gu, w_down):
                gu = w_gu[0].rearrange("(k p) n -> p k n", p=P)
                down = w_down[0].rearrange("(k p) n -> p k n", p=P)
                first = 1 if c0 == 0 else 0
                for p in range(first):
                    for j in range(2):
                        load(c0 + j, (c0 + j) % 2, by_rows((c0 + j) % 2, gu[:, :, j * FF:j * FF + CW], DK))
                with sp.Fori(first, GU) as p:
                    for j in range(2):
                        slot = (c0 + j) % 2
                        load(p * 2 + (c0 + j), slot,
                             by_rows(slot, gu[:, :, bass.ds(p * CW + j * FF, CW)], DK))
                d0 = c0 + 2 * GU
                with sp.Fori(0, NPAIR) as n:
                    for j, (k0, kb) in enumerate(zip(DOWN_K0, DOWN_KB)):
                        slot = (d0 + j) % 2
                        load(n * 4 + (d0 + j), slot,
                             by_rows(slot, down[:, k0:k0 + kb, bass.ds(n * CW, CW)], kb))

            for i in range(QT):
                sp.dma_start(xin[:, i, :], x[0, i * P:(i + 1) * P, :]).then_inc(x_in[i], 16)
            load_ffn(0, w_ffn1_gu, w_ffn1_down)

            win = w_in[0].rearrange("(k p) n -> p k n", p=P)
            wa = w_branch_a[0].rearrange("(k p) n -> p k n", p=P)
            wb = w_branch_b[0].rearrange("(g t p) n -> g p t n", g=2, t=4)
            wo = w_out[0].rearrange("(k p) n -> p k n", p=P)
            col0 = {"qa": QA0, "ka": KA0, "va": VA0, "kvb": KVB0, "ga": GA0, "gb": GB0}
            for n, (kind, i, kb) in enumerate(MIX):
                c = C_MIX + n
                slot = c % 2
                cols = slice(i * CW, (i + 1) * CW)
                if kind == "qb":
                    halves = []
                    for j in range(2):
                        for g in range(2):
                            c1 = QB0 + (2 * i + j + 4 * g) * HD
                            halves.append((raw[:, slot, :, (2 * j + g) * HD:(2 * j + g + 1) * HD],
                                           win[:, :, c1:c1 + HD]))
                elif kind == "ya":
                    halves = by_rows(slot, wa[:, :, cols], kb)
                elif kind == "yb":
                    halves = [(raw[g * HD:(g + 1) * HD, slot, 0:kb, :], wb[g][:, :, cols]) for g in range(2)]
                elif kind == "out":
                    halves = by_rows(slot, wo[:, :, cols], kb)
                else:
                    c1 = col0[kind] + i * CW
                    halves = by_rows(slot, win[:, :, c1:c1 + CW], kb)
                load(c, slot, halves)
            load_ffn(C_FFN2, w_ffn2_gu, w_ffn2_down)

            sp.wait_ge(used, used_at(N_CHUNKS - 1))
            sp.dma_start(g_fin[:, :], g_final.partition_broadcast(P)).then_inc(fin_in, 16)
            for i in range(QT):
                sp.wait_ge(y_done, i + 1)
                sp.dma_start(out[0, i * P:(i + 1) * P, :], xs[:, i, :]).then_inc(out_done, 16)
            sp.wait_ge(out_done, 16 * QT)

        @block.gpsimd
        def _(pl):
            pl.dma_start(ident[:, :], identity).then_inc(consts_in, 16)
            with nc.allow_non_contiguous_dma(reason="3072 gains, once"):
                for n, g in enumerate((g_ffn1, g_mix, g_ffn2)):
                    pl.dma_start(gains[:, n, :], g[0].rearrange("(k p) -> p k", p=P)).then_inc(consts_in, 16)
            pl.dma_start(sinks[:, :], b_sinks[0].partition_broadcast(P)).then_inc(consts_in, 16)
            pl.dma_start(relrow[:, :], a_rel_bias[0]).then_inc(consts_in, 16)
            pl.memset(ones[:, :], 1.0).then_inc(ones_set, 1)
            pl.memset(eps[:, :], EPS).then_inc(ones_set, 1)
            pl.wait_ge(ext_set, 2)
            pl.dma_start(ext_dram[:, :], extrow[:, :]).then_inc(ext_out, 16)
            pl.wait_ge(ext_out, 16)
            pl.wait_ge(norm_lo, DK)
            pl.dma_start(cs[:, :, :], rope).then_inc(consts_in, 16)
            pl.memset(f32(vv[:, :, :, :, 1, :]).rearrange("p a b c d -> p (a b c) d"), 0.0).then_inc(zeros_set, 1)
            pl.memset(mask_b[:, :], 0.0).then_inc(pool, 1)
            pl.wait_ge(pool, 1)
            pl.memset(mask_b[0:CH, 0:CH], MASKED).then_inc(pool, 1)
            pl.memset(mask_b[0:CH, 3 * CH:4 * CH], MASKED).then_inc(pool, 1)
            pl.memset(mask_b[CH:P, 0:2 * CH], MASKED).then_inc(zeros_set, 1)
            pl.wait_ge(pool, 3)
            for s in range(HEADS):
                if s >= 2:
                    pl.wait_ge(s_used, 4 * (s - 1))
                src = bass.AP(ext_dram, s * EXT, [[1, P], [1, S]])
                pl.dma_start(bias_a[:, s % 2, :], src).then_inc(bias_in, 16)
                pl.wait_ge(bias_in, 16 * (s + 1))
                pl.memset(bias_a[0:CH, s % 2, 0:CH], MASKED).then_inc(bias_ready, 1)

        @block.scalar
        def _(act):
            n_own = [0]

            def split(c, slot, kb):
                act.wait_ge(raw_in[slot], loaded_at(c))
                if c >= 2:
                    wait_used(act, c - 2)
                nc.scalar.activation(w_hl[:, slot, 0, 0:kb, :], raw[:, slot, 0:kb, :],
                                     ACT.Copy).then_inc(hi_done, 1)

            def split_at(c_of, reg, slot, kb):
                per, base = c_of
                act.wait_ge(raw_in[slot], reg * (16 * per) + loaded_at(base))
                act.wait_ge(used, reg * per + used_at(base - 2))
                nc.scalar.activation(w_hl[:, slot, 0, 0:kb, :], raw[:, slot, 0:kb, :],
                                     ACT.Copy).then_inc(hi_done, 1)

            act.wait_ge(ones_set, 2)
            for i in range(QT):
                act.wait_ge(x_in[i], 16)
                if i:
                    act.wait_ge(sq_done, i)
                nc.scalar.activation(junk[:, :], xin[:, i, :], ACT.Square,
                                     accum_out=stat[:, i:i + 1]).then_inc(sq_done, 1)
            act.wait_ge(sq_done, QT)
            nc.scalar.activation(stat[:, 4:8], stat[:, 0:4], ACT.Sqrt, bias=eps[:, :],
                                 scale=1.0 / D).then_inc(rms_done, 1)
            split(0, 0, DK)
            act.wait_ge(consts_in, 16 * 6)
            for f in range(DK):
                act.wait_ge(xt_done, f + 1)
                nc.scalar.activation(xn[:, 0, f, :], pj[:, f % 4, :], ACT.Copy,
                                     scale=gains[:, 0, f:f + 1]).then_inc(xt_hi, 1)
            split(1, 1, DK)

            def ffn_act(c0, f):
                def gate(p):
                    if f or not isinstance(p, int) or p:
                        act.wait_ge(gated, p + f * GU)
                    act.wait_ge(used, p * 2 + used_at(c0))
                    nc.scalar.activation(silu[:, :, :], pj[:, 0:2, :], ACT.Silu).then_inc(silu_done, 1)

                def hidden(p):
                    act.wait_ge(gated, p + (f * GU + 1))
                    nc.scalar.activation(hid[:, 0, bass.ds(p * 2, 2), :], work[:, :, :],
                                         ACT.Copy).then_inc(hid_hi, 1)

                gate(0)
                with act.Fori(0, GU - 1) as p:
                    split_at((2, c0 + 2), p, c0 % 2, DK)
                    hidden(p)
                    split_at((2, c0 + 3), p, (c0 + 1) % 2, DK)
                    gate(p + 1)
                d0 = c0 + 2 * GU
                split(d0, d0 % 2, DOWN_KB[0])
                hidden(GU - 1)
                with act.Fori(0, NPAIR - 1) as n:
                    for j in range(4):
                        split_at((4, d0 + 1 + j), n, (d0 + 1 + j) % 2, DOWN_KB[(j + 1) % 4])
                    if f == 0:
                        act.wait_ge(h_done, n + 1)
                        nc.scalar.activation(silu[:, :, :], h[:, bass.ds(n * 2, 2), :],
                                             ACT.Square).then_inc(sq_pair, 1)
                        act.wait_ge(acc_done, n + 1)
                dl = d0 + 4 * (NPAIR - 1)
                for j in range(1, 4):
                    split(dl + j, (dl + j) % 2, DOWN_KB[j])
                if f == 0:
                    split(dl + 4, (dl + 4) % 2, kb_of(dl + 4))
                    act.wait_ge(h_done, NPAIR)
                    nc.scalar.activation(silu[:, :, :], h[:, 2 * NPAIR - 2:2 * NPAIR, :],
                                         ACT.Square).then_inc(sq_pair, 1)

            def norm_act(n):
                act.wait_ge(ms_done, n + 1)
                nc.scalar.activation(norm_s[:, 1, :], po[:, 0, :], ACT.Sqrt, bias=eps[:, :],
                                     scale=1.0 / D).then_inc(rms_sqrt, 1)
                for k in range(DK):
                    act.wait_ge(norm_t, DK * n + k + 1)
                    nc.scalar.activation(xn[:, 0, k, :], work[:, k % 2, :], ACT.Copy).then_inc(norm_hi, 1)

            ffn_act(0, 0)
            norm_act(0)

            def start_chunk(c):
                c += C_MIX + 1
                split(c, c % 2, kb_of(c))

            def copy_hi(dst, src):
                return nc.scalar.activation(dst, src, ACT.Copy)

            def evacuate(tau):
                kind, i, m = tile_kind(tau)
                bank = pj[:, tau % 2, :]
                t = 2 * i + m
                if kind in ("qa", "ka"):
                    act.wait_ge(tile_done, tau + 1)
                    copy_hi((qa if kind == "qa" else kk)[:, t, 0, :], bank).then_inc(split_hi, 1)
                elif kind == "va":
                    act.wait_ge(tile_done, tau + 1)
                    for j in range(2):
                        src = bank[:, j * CW:(j + 1) * CW].rearrange("p (a b d) -> p a b d", a=2, b=2)
                        last = copy_hi(vv[:, 2 * i:2 * i + 2, 0, 2 * m + j, 0:3:2, :], src)
                    last.then_inc(split_hi, 1)
                elif kind == "vb":
                    act.wait_ge(tile_done, tau + 1)
                    src = bank.rearrange("p (t b d) -> p t b d", t=QT, b=2)
                    copy_hi(vv[:, 0, 0, :, 0:3:2, :], src).then_inc(split_hi, 1)
                elif kind in ("qb", "kb"):
                    act.wait_ge(rope_sum, ROPED.index(tau) + 1)
                    copy_hi(qb[:, t, 0, :] if kind == "qb" else kk[:, 0, 0, :],
                            roped[:, 0, :]).then_inc(split_hi, 1)
                elif kind in ("ga", "gb"):
                    act.wait_ge(tile_done, tau + 1)
                    n = GATES.index(tau)
                    if n == 0:
                        act.wait_ge(roped_lo, len(ROPED))
                    if n >= 2:
                        act.wait_ge(tile_free[(tau - 2) % 2], (tau - 2) // 2 + 1)
                    nc.scalar.activation(norm_s[:, n % 2, :], bank, ACT.Exp, scale=-1.0).then_inc(gate_exp, 1)
                elif kind == "yb":
                    act.wait_ge(merged_sum, MERGED.index(tau) + 1)
                    copy_hi(qa[:, t // 2, t % 2, :], sc[:, 0:S]).then_inc(split_hi, 1)

            def output_hi(pr):
                act.wait_ge(pv_done, 2 * pr + 2)
                copy_hi((qa if pr < 4 else qb)[:, pr % 4, 0, :], po[:, pr % 2, :]).then_inc(o_hi, 1)

            tau = 0
            for c, m in BEFORE:
                if m == 0:
                    start_chunk(c)
                evacuate(tau)
                tau += 1
            for s in range(NH):
                kind_b = s >= HEADS
                at = 0
                for i in range(QT):
                    u = QT * s + i
                    _, n = n_keys(s, i)
                    act.wait_ge(neg_done, u + 1)
                    own = nc.scalar.activation(sc[:, at:at + n], sc[:, at:at + n], ACT.Exp,
                                               bias=stat[:, 4 + i:5 + i], accum_out=rows[:, i:i + 1])
                    if kind_b:
                        hq = (s - HEADS) // 2 + 4 * (s % 2)
                        own.then_inc(actc, 1)
                        nc.scalar.activation(stat[:, i:i + 1], sinks[:, hq:hq + 1], ACT.Exp,
                                             bias=stat[:, 4 + i:5 + i]).then_inc(exp_done, 1)
                    else:
                        own.then_inc(exp_done, 1)
                    at += n
                if s and s % 2 == 0:
                    output_hi(s // 2 - 1)
                for c, m in FILL[s]:
                    if m == 0:
                        start_chunk(c)
                    evacuate(tau)
                    tau += 1
                for i in range(QT):
                    u = QT * s + i
                    first, n = n_keys(s, i)
                    j0, nj = first // P, n // P
                    act.wait_ge(t_done, u + 1)
                    if s:
                        act.wait_ge(pv_done, s)
                    copy_hi(pt[:, 0, j0:j0 + nj, i * P:(i + 1) * P],
                            pj[:, 2 + u % 2, 0:n].rearrange("p (j q) -> p j q", q=P)).then_inc(pt_hi, 1)
            output_hi(NH // 2 - 1)
            for c, m in AFTER:
                if m == 0:
                    start_chunk(c)
                evacuate(tau)
                tau += 1
            for n in range(NPAIR):
                c = C_OUT + n + 1
                split(c, c % 2, kb_of(c))
                act.wait_ge(h_done, NPAIR + n + 1)
                if n:
                    act.wait_ge(acc_done, NPAIR + n)
                nc.scalar.activation(silu[:, :, :], h[:, 2 * n:2 * n + 2, :], ACT.Square).then_inc(sq_pair, 1)
            norm_act(1)
            split(C_FFN2 + 1, (C_FFN2 + 1) % 2, DK)
            ffn_act(C_FFN2, 1)

            for i in range(QT):
                act.wait_ge(yt_used, 2 * (i + 1))
                if i:
                    act.wait_ge(sq_done, QT + i)
                nc.scalar.activation(junk[:, :], xin[:, i, :], ACT.Square,
                                     accum_out=stat[:, i:i + 1]).then_inc(sq_done, 1)
            act.wait_ge(sq_done, 2 * QT)
            nc.scalar.activation(stat[:, 4:8], stat[:, 0:4], ACT.Sqrt, bias=eps[:, :],
                                 scale=1.0 / D).then_inc(rms_done, 1)

        @block.vector
        def _(ve):
            own = [0]

            def link(ins):
                own[0] += 1
                ins.then_inc(dve, 1)
                ve.wait_ge(dve, own[0])

            def minus_hi(dst, src, hi):
                return nc.vector.tensor_tensor(dst, src, f32(hi), ALU.subtract)

            def split(c, slot, kb):
                ve.wait_ge(hi_done, c + 1)
                minus_hi(w_hl[:, slot, 1, 0:kb, :], raw[:, slot, 0:kb, :],
                         w_hl[:, slot, 0, 0:kb, :]).then_inc(lo_done, 1)

            ve.wait_ge(rms_done, 1)
            link(nc.vector.reciprocal(rows[:, 0:4], stat[:, 4:8]))
            for i in range(QT):
                nc.vector.tensor_scalar(xs[:, i, :], xin[:, i, :], rows[:, i:i + 1], None,
                                        ALU.mult).then_inc(xs_done, 1)
            split(0, 0, DK)
            for f in range(DK):
                ve.wait_ge(xt_hi, f + 1)
                nc.vector.scalar_tensor_tensor(xn[:, 1, f, :], pj[:, f % 4, :], gains[:, 0, f:f + 1],
                                               f32(xn[:, 0, f, :]), ALU.mult, ALU.subtract).then_inc(xt_lo, 1)
            for f in range(DK):
                ve.wait_ge(ht_done, f + 1)
                nc.vector.tensor_copy(h[:, f, :], po[:, f % 2, :]).then_inc(ht_used, 1)
            ve.wait_ge(consts_in, 16 * 6)
            near = P + MAX_REL - 1
            nc.vector.tensor_scalar(extrow[:, 0:near], relrow[:, 1:near + 1], 1.0 / SCALE, None,
                                    ALU.mult).then_inc(ext_set, 1)
            link(nc.vector.memset(extrow[:, near:EXT], 1.0 / SCALE))
            nc.vector.tensor_scalar(extrow[:, near:EXT], extrow[:, near:EXT],
                                    relrow[:, 2 * MAX_REL:2 * MAX_REL + 1], None, ALU.mult).then_inc(ext_set, 1)
            ve.wait_ge(ext_out, 16)
            split(1, 1, DK)

            def ffn_dve(c0, f):
                def product(p):
                    ve.wait_ge(silu_done, p + (f * GU + 1))
                    ve.wait_ge(used, p * 2 + used_at(c0 + 1))
                    nc.vector.tensor_tensor(work[:, :, :], silu[:, :, :], pj[:, 2:4, :],
                                            ALU.mult).then_inc(gated, 1)

                def hidden_lo(p):
                    ve.wait_ge(hid_hi, p + (f * GU + 1))
                    minus_hi(hid[:, 1, bass.ds(p * 2, 2), :], work[:, :, :],
                             hid[:, 0, bass.ds(p * 2, 2), :]).then_inc(hid_lo, 1)

                with ve.Fori(0, GU - 1) as p:
                    split(p * 2 + (c0 + 2), c0 % 2, DK)
                    product(p)
                    hidden_lo(p)
                    split(p * 2 + (c0 + 3), (c0 + 1) % 2, DK)
                d0 = c0 + 2 * GU
                split(d0, d0 % 2, DOWN_KB[0])
                product(GU - 1)
                hidden_lo(GU - 1)
                if f == 0:
                    link(nc.vector.memset(norm_s[:, 0, :], 0.0))

                def add(n, pair):
                    ve.wait_ge(used, n * 4 + used_at(d0 + 3))
                    nc.vector.scalar_tensor_tensor(h[:, bass.ds(n * 2, 2), :], pj[:, pair:pair + 2, :], 0.5,
                                                   h[:, bass.ds(n * 2, 2), :], ALU.mult,
                                                   ALU.add).then_inc(h_done, 1)

                def sums(n):
                    ve.wait_ge(sq_pair, n + 1)
                    link(nc.vector.tensor_tensor(norm_s[:, 0, :], norm_s[:, 0, :], silu[:, 0, :], ALU.add))
                    nc.vector.tensor_tensor(norm_s[:, 0, :], norm_s[:, 0, :], silu[:, 1, :],
                                            ALU.add).then_inc(acc_done, 1)
                    ve.wait_ge(acc_done, n + 1)

                for n in range(NPAIR):
                    for j in range(1, 4 if n == NPAIR - 1 else 5):
                        c = d0 + 4 * n + j
                        split(c, c % 2, kb_of(c))
                    if f == 0 and n == NPAIR - 1:
                        c = d0 + 4 * NPAIR
                        split(c, c % 2, kb_of(c))
                    add(n, 2 * (n % 2))
                    if f == 0:
                        sums(n)

            def norm_dve(n):
                ve.wait_ge(rms_sqrt, n + 1)
                link(nc.vector.reciprocal(norm_s[:, 1, :], norm_s[:, 1, :]))

                def scaled(k):
                    nc.vector.scalar_tensor_tensor(work[:, k % 2, :], h[:, k, :], gains[:, n + 1, k:k + 1],
                                                   norm_s[:, 1, :], ALU.mult, ALU.mult).then_inc(norm_t, 1)

                def low(k):
                    ve.wait_ge(norm_hi, DK * n + k + 1)
                    minus_hi(xn[:, 1, k, :], work[:, k % 2, :], xn[:, 0, k, :]).then_inc(norm_lo, 1)
                    ve.wait_ge(norm_lo, DK * n + k + 1)

                scaled(0)
                for k in range(1, DK):
                    scaled(k)
                    low(k - 1)
                low(DK - 1)

            ffn_dve(0, 0)
            norm_dve(0)

            def start_chunk(c):
                c += C_MIX + 1
                split(c, c % 2, kb_of(c))

            def evacuate(tau):
                kind, i, m = tile_kind(tau)
                bank = pj[:, tau % 2, :]
                free = tile_free[tau % 2]
                t = 2 * i + m
                if kind in ("qa", "ka"):
                    dst = qa if kind == "qa" else kk
                    ve.wait_ge(split_hi, SPLIT.index(tau) + 1)
                    minus_hi(dst[:, t, 1, :], bank, dst[:, t, 0, :]).then_inc(free, 1)
                elif kind == "va":
                    ve.wait_ge(split_hi, SPLIT.index(tau) + 1)
                    for j in range(2):
                        src = bank[:, j * CW:(j + 1) * CW].rearrange("p (a b d) -> p a b d", a=2, b=2)
                        last = minus_hi(vv[:, 2 * i:2 * i + 2, 1, 2 * m + j, 0:3:2, :], src,
                                        vv[:, 2 * i:2 * i + 2, 0, 2 * m + j, 0:3:2, :])
                    last.then_inc(free, 1)
                elif kind == "vb":
                    ve.wait_ge(split_hi, SPLIT.index(tau) + 1)
                    src = bank.rearrange("p (t b d) -> p t b d", t=QT, b=2)
                    minus_hi(vv[:, 0, 1, :, 0:3:2, :], src, vv[:, 0, 0, :, 0:3:2, :]).then_inc(free, 1)
                elif kind in ("qb", "kb"):
                    ve.wait_ge(consts_in, 16 * 7)
                    ve.wait_ge(tile_done, tau + 1)
                    for q in range(4):
                        o = q ^ 1
                        last = nc.vector.tensor_tensor(roped[32 * q:32 * q + 32, 1, :], bank[32 * o:32 * o + 32, :],
                                                       cs[32 * o:32 * o + 32, 1, :], ALU.mult)
                    link(last)
                    nc.vector.tensor_tensor(roped[:, 0, :], bank, cs[:, 0, :], ALU.mult).then_inc(free, 1)
                    ve.wait_ge(free, tau // 2 + 1)
                    nc.vector.tensor_tensor(roped[:, 0, :], roped[:, 0, :], roped[:, 1, :],
                                            ALU.add).then_inc(rope_sum, 1)
                    dst = qb[:, t, :, :] if kind == "qb" else kk[:, 0, :, :]
                    ve.wait_ge(split_hi, SPLIT.index(tau) + 1)
                    minus_hi(dst[:, 1, :], roped[:, 0, :], dst[:, 0, :]).then_inc(roped_lo, 1)
                elif kind in ("ga", "gb"):
                    n = GATES.index(tau)
                    ve.wait_ge(gate_exp, n + 1)
                    g = norm_s[:, n % 2, :]
                    link(nc.vector.tensor_scalar(g, g, 1.0, None, ALU.add))
                    nc.vector.reciprocal(g, g).then_inc(free, 1)
                    ve.wait_ge(free, tau // 2 + 1)
                elif kind == "ya":
                    ve.wait_ge(tile_done, tau + 1)
                    nc.vector.tensor_tensor(y_gated[:, t, :], norm_s[:, m, :], bank, ALU.mult).then_inc(free, 1)
                elif kind == "yb":
                    ve.wait_ge(tile_done, tau + 1)
                    n = MERGED.index(tau)
                    if n:
                        ve.wait_ge(merged_lo, n)
                    nc.vector.tensor_tensor(sc[:, 0:S], norm_s[:, m, :], bank, ALU.mult).then_inc(free, 1)
                    ve.wait_ge(free, tau // 2 + 1)
                    nc.vector.tensor_tensor(sc[:, 0:S], sc[:, 0:S], y_gated[:, t, :],
                                            ALU.add).then_inc(merged_sum, 1)
                    ve.wait_ge(split_hi, SPLIT.index(tau) + 1)
                    minus_hi(pt[:, t // 4, t % 4, :], sc[:, 0:S], qa[:, t // 2, t % 2, :]).then_inc(merged_lo, 1)

            def output_lo(pr):
                dst = qa if pr < 4 else qb
                ve.wait_ge(o_hi, pr + 1)
                minus_hi(dst[:, pr % 4, 1, :], po[:, pr % 2, :], dst[:, pr % 4, 0, :]).then_inc(o_lo, 1)

            tau = 0
            for c, m in BEFORE:
                if m == 0:
                    start_chunk(c)
                evacuate(tau)
                tau += 1
            for s in range(NH):
                b = s >= HEADS
                hq = (s - HEADS) // 2 + 4 * (s % 2)
                if s == 0:
                    ve.wait_ge(zeros_set, 2)
                if not b:
                    ve.wait_ge(bias_ready, s + 1)
                at = 0
                spans = []
                for i in range(QT):
                    u = QT * s + i
                    _, n = n_keys(s, i)
                    ve.wait_ge(s_done, u + 1)
                    if s:
                        ve.wait_ge(t_done, QT * s)
                    table = mask_b[:, 2 * P - n:2 * P] if b else bias_a[:, s % 2, n - 1::-1]
                    nc.vector.tensor_tensor_reduce(sc[:, at:at + n], ps[:, u % 2, 0:n], table, SCALE, MASKED,
                                                   ALU.add, ALU.max, rows[:, i:i + 1]).then_inc(s_used, 1)
                    ve.wait_ge(s_used, u + 1)
                    if b:
                        nc.vector.tensor_scalar(stat[:, 4 + i:5 + i], rows[:, i:i + 1], sinks[:, hq:hq + 1], -1.0,
                                                ALU.max, ALU.mult).then_inc(neg_done, 1)
                    else:
                        nc.vector.tensor_scalar(stat[:, 4 + i:5 + i], rows[:, i:i + 1], -1.0, None,
                                                ALU.mult).then_inc(neg_done, 1)
                    spans.append((at, n))
                    at += n
                for i, (at, n) in enumerate(spans):
                    ve.wait_ge(exp_done, QT * s + i + 1)
                    if b:
                        ve.wait_ge(actc, QT * (s - HEADS) + i + 1)
                        link(nc.vector.tensor_tensor(rows[:, i:i + 1], rows[:, i:i + 1], stat[:, i:i + 1], ALU.add))
                    link(nc.vector.reciprocal(rows[:, i:i + 1], rows[:, i:i + 1]))
                    nc.vector.tensor_scalar(sc[:, at:at + n], sc[:, at:at + n], rows[:, i:i + 1], None,
                                            ALU.mult).then_inc(p_done, 1)
                if s and s % 2 == 0:
                    output_lo(s // 2 - 1)
                for c, m in FILL[s]:
                    if m == 0:
                        start_chunk(c)
                    evacuate(tau)
                    tau += 1
                for i in range(QT):
                    u = QT * s + i
                    first, n = n_keys(s, i)
                    j0, nj = first // P, n // P
                    ve.wait_ge(pt_hi, u + 1)
                    cut = (slice(None), slice(j0, j0 + nj), slice(i * P, (i + 1) * P))
                    minus_hi(pt[:, 1, :, :][cut], pj[:, 2 + u % 2, 0:n].rearrange("p (j q) -> p j q", q=P),
                             pt[:, 0, :, :][cut]).then_inc(pt_lo, 1)
            output_lo(NH // 2 - 1)
            for c, m in AFTER:
                if m == 0:
                    start_chunk(c)
                evacuate(tau)
                tau += 1
            link(nc.vector.memset(norm_s[:, 0, :], 0.0))
            for n in range(NPAIR):
                c = C_OUT + n + 1
                split(c, c % 2, kb_of(c))
                wait_used(ve, C_OUT + n)
                pair = 2 * (n % 2)
                nc.vector.tensor_tensor(h[:, 2 * n:2 * n + 2, :], pj[:, pair:pair + 2, :], h[:, 2 * n:2 * n + 2, :],
                                        ALU.add).then_inc(h_done, 1)
                ve.wait_ge(sq_pair, NPAIR + n + 1)
                link(nc.vector.tensor_tensor(norm_s[:, 0, :], norm_s[:, 0, :], silu[:, 0, :], ALU.add))
                nc.vector.tensor_tensor(norm_s[:, 0, :], norm_s[:, 0, :], silu[:, 1, :], ALU.add).then_inc(acc_done, 1)
                ve.wait_ge(acc_done, NPAIR + n + 1)
            norm_dve(1)
            split(C_FFN2 + 1, (C_FFN2 + 1) % 2, DK)
            ffn_dve(C_FFN2, 1)

            ve.wait_ge(used, used_at(N_CHUNKS - 1))
            for n in range(2 * QT):
                ve.wait_ge(yt_done, n + 1)
                nc.vector.tensor_copy(xin[:, n // 2, (n % 2) * S:(n % 2 + 1) * S], po[:, n % 2, :]).then_inc(yt_used, 1)
            ve.wait_ge(rms_done, 2)
            link(nc.vector.reciprocal(rows[:, 0:4], stat[:, 4:8]))
            ve.wait_ge(fin_in, 16)
            for i in range(QT):
                nc.vector.scalar_tensor_tensor(xs[:, i, :], xin[:, i, :], rows[:, i:i + 1], g_fin[:, :],
                                               ALU.mult, ALU.mult).then_inc(y_done, 1)

        @block.tensor
        def _(pe):
            def project(out_banks, slot, kb, moving, start=True, stop=True, ready=None):
                for k in range(kb):
                    if ready:
                        ready(k)
                    for m in range(2):
                        for wh, xh in PRODUCTS:
                            last = nc.tensor.matmul(out_banks[:, m, :], w_hl[:, slot, wh, k, m * P:(m + 1) * P],
                                                    moving(xh, k), start=start and k == 0 and (wh, xh) == (0, 0),
                                                    stop=stop and k == kb - 1 and (wh, xh) == PRODUCTS[-1])
                return last

            def of_xn(xh, k):
                return xn[:, xh, k, :]

            pe.wait_ge(consts_in, 16 * 6)
            pe.wait_ge(xs_done, QT)
            for f in range(DK):
                if f >= 4:
                    pe.wait_ge(xt_lo, f - 3)
                for i in range(QT):
                    last = nc.tensor.transpose(pj[:, f % 4, i * P:(i + 1) * P], xs[:, i, f * P:(f + 1) * P],
                                               ident[:, :])
                last.then_inc(xt_done, 1)
            for f in range(DK):
                if f >= 2:
                    pe.wait_ge(ht_used, f - 1)
                for i in range(QT):
                    last = nc.tensor.transpose(po[:, f % 2, i * P:(i + 1) * P], xin[:, i, f * P:(f + 1) * P],
                                               ident[:, :])
                last.then_inc(ht_done, 1)

            def ffn_pe(c0, f, xn_ready):
                def gate(p, ready=None):
                    pe.wait_ge(lo_done, p * 2 + (c0 + 1))
                    if not isinstance(p, int) or p:
                        pe.wait_ge(silu_done, p + f * GU)
                    project(pj[:, 0:2, :], c0 % 2, DK, of_xn, ready=ready).then_inc(used, 1)

                def up(p):
                    pe.wait_ge(lo_done, p * 2 + (c0 + 2))
                    if not isinstance(p, int) or p:
                        pe.wait_ge(gated, p + f * GU)
                    project(pj[:, 2:4, :], (c0 + 1) % 2, DK, of_xn).then_inc(used, 1)

                gate(0, xn_ready)
                up(0)
                with pe.Fori(1, GU) as p:
                    gate(p)
                    up(p)
                d0 = c0 + 2 * GU
                for n in range(NPAIR):
                    pair = 2 * (n % 2)
                    for j, (k0, kb) in enumerate(zip(DOWN_K0, DOWN_KB)):
                        c = d0 + 4 * n + j
                        pe.wait_ge(lo_done, c + 1)
                        if n == 0 and j == 0:
                            pe.wait_ge(silu_done, (f + 1) * GU)
                        if n == 0 and j == 3:
                            pe.wait_ge(hid_lo, (f + 1) * GU)
                        elif n == 0:
                            pe.wait_ge(hid_lo, f * GU + (k0 + kb + 1) // 2)
                        if j == 0 and n == 1:
                            pe.wait_ge(gated, (f + 1) * GU)
                        if j == 0 and n >= 2:
                            pe.wait_ge(h_done, 2 * NPAIR * f + n - 1)
                        project(pj[:, pair:pair + 2, :], c % 2, kb, lambda xh, k, k0=k0: hid[:, xh, k0 + k, :],
                                start=j == 0, stop=j == 3).then_inc(used, 1)

            def norm_pe(n):
                pe.wait_ge(acc_done, NPAIR * (n + 1))
                nc.tensor.matmul(po[:, 0, :], ones[:, :], norm_s[:, 0, :], start=True, stop=True).then_inc(ms_done, 1)

            def first_ready(k):
                pe.wait_ge(xt_lo, k + 1)
                if k == 0:
                    pe.wait_ge(xt_lo, DK - 2)

            ffn_pe(0, 0, first_ready)
            norm_pe(0)

            def tile(tau):
                c, m = TILES[tau]
                kind, i, mm = tile_kind(tau)
                slot = (C_MIX + c) % 2
                bank = pj[:, tau % 2, :]
                if m == 0:
                    pe.wait_ge(lo_done, C_MIX + c + 1)
                if tau >= 2:
                    pe.wait_ge(tile_free[tau % 2], tau // 2)
                else:
                    pe.wait_ge(h_done, NPAIR)
                kb = MIX[c][2]
                w = w_hl[:, slot, :, :, :]
                if kind in ("va", "vb"):
                    width = CW if kind == "va" else P
                    tiles = (2 * m, 2 * m + 1) if kind == "va" else range(QT)
                    for n, t in enumerate(tiles):
                        for k in range(kb):
                            for xh, wh in PRODUCTS:
                                last = nc.tensor.matmul(bank[:, n * width:(n + 1) * width],
                                                        xn[:, xh, k, t * P:(t + 1) * P],
                                                        w[:, wh, k, CW - width:CW],
                                                        start=k == 0 and (xh, wh) == (0, 0),
                                                        stop=k == kb - 1 and (xh, wh) == PRODUCTS[-1])
                else:
                    if tau == 0:
                        ready = lambda k: pe.wait_ge(norm_lo, k + 1)
                    else:
                        ready = lambda k: None
                    if kind == "ya" and m == 0 and i == 0:
                        pe.wait_ge(o_lo, 4)
                    if kind == "yb" and m == 0 and i == 0:
                        pe.wait_ge(o_lo, 8)
                    for k in range(kb):
                        ready(k)
                        for wh, xh in PRODUCTS:
                            lhs = w[:, wh, k, m * P:(m + 1) * P]
                            rhs = (qa[:, k, xh, :] if kind == "ya" else qb[:, k, xh, :] if kind == "yb"
                                   else xn[:, xh, k, :])
                            last = nc.tensor.matmul(bank, lhs, rhs, start=k == 0 and (wh, xh) == (0, 0),
                                                    stop=k == kb - 1 and (wh, xh) == PRODUCTS[-1])
                last.then_inc(tile_done, 1)

            def scores(s):
                b = s >= HEADS
                t, a = (s % HEADS) // 2, s % 2
                q, kt = (qb, 0) if b else (qa, t)
                r = slice(a * HD, (a + 1) * HD)
                need = [x for x in range(len(TILES)) if
                        (tile_kind(x)[0] == ("qb" if b else "qa") and 2 * tile_kind(x)[1] + tile_kind(x)[2] == t)
                        or (tile_kind(x)[0] == "kb" if b else
                            (tile_kind(x)[0] == "ka" and 2 * tile_kind(x)[1] + tile_kind(x)[2] == t))]
                for x in need:
                    if tile_kind(x)[0] in ("qb", "kb"):
                        pe.wait_ge(roped_lo, ROPED.index(x) + 1)
                    else:
                        pe.wait_ge(tile_free[x % 2], x // 2 + 1)
                for i in range(QT):
                    u = QT * s + i
                    first, n = n_keys(s, i)
                    if u >= 2:
                        pe.wait_ge(s_used, u - 1)
                    for qh, kh in PRODUCTS:
                        last = nc.tensor.matmul(ps[:, u % 2, 0:n], q[r, t, qh, i * P:(i + 1) * P],
                                                kk[r, kt, kh, first:first + n],
                                                start=(qh, kh) == (0, 0), stop=(qh, kh) == PRODUCTS[-1])
                    last.then_inc(s_done, 1)

            def transposes(s):
                at = 0
                for i in range(QT):
                    u = QT * s + i
                    _, n = n_keys(s, i)
                    pe.wait_ge(p_done, u + 1)
                    if u >= 2:
                        pe.wait_ge(pt_lo, u - 1)
                    for j in range(n // P):
                        last = nc.tensor.transpose(pj[:, 2 + u % 2, j * P:(j + 1) * P],
                                                   sc[:, at + j * P:at + (j + 1) * P], ident[:, :])
                    last.then_inc(t_done, 1)
                    at += n

            def values(s):
                b = s >= HEADS
                pr, a = s // 2, s % 2
                vt = 0 if b else pr
                pe.wait_ge(pt_lo, QT * (s + 1))
                if s == 0:
                    pe.wait_ge(zeros_set, 1)
                vneed = [x for x in range(len(TILES)) if tile_kind(x)[0] == ("vb" if b else "va")
                         and (b or tile_kind(x)[1] == pr // 2)]
                for x in vneed:
                    pe.wait_ge(tile_free[x % 2], x // 2 + 1)
                if a == 0 and pr >= 2:
                    pe.wait_ge(o_lo, pr - 1)
                for j in range(QT):
                    q1 = min(S, (j + 2) * P) if b else S
                    for vh, ph in PRODUCTS:
                        last = nc.tensor.matmul(po[:, pr % 2, j * P:q1],
                                                vv[:, vt, vh, j, a:a + 2, :], pt[:, ph, j, j * P:q1],
                                                start=a == 0 and j == 0 and (vh, ph) == (0, 0),
                                                stop=a == 1 and j == QT - 1 and (vh, ph) == PRODUCTS[-1],
                                                skip_group_check=True)
                last.then_inc(pv_done, 1)

            tau = 0
            for _x in BEFORE:
                tile(tau)
                tau += 1
            scores(0)
            for s in range(NH):
                for _x in FILL[s]:
                    tile(tau)
                    tau += 1
                transposes(s)
                if s + 1 < NH:
                    scores(s + 1)
                values(s)
            for _x in AFTER:
                tile(tau)
                tau += 1
            for n in range(NPAIR):
                c = C_OUT + n
                pair = 2 * (n % 2)
                pe.wait_ge(lo_done, c + 1)
                if n == 0:
                    pe.wait_ge(merged_lo, len(MERGED))
                if n >= 2:
                    pe.wait_ge(h_done, NPAIR + n - 1)
                project(pj[:, pair:pair + 2, :], c % 2, DK,
                        lambda xh, k: pt[:, k // 4, k % 4, :] if xh else qa[:, k // 2, k % 2, :]).then_inc(used, 1)
            norm_pe(1)

            def second_ready(k):
                pe.wait_ge(norm_lo, DK + k + 1)
            ffn_pe(C_FFN2, 1, second_ready)

            pe.wait_ge(h_done, 3 * NPAIR)
            for n in range(2 * QT):
                if n >= 2:
                    pe.wait_ge(yt_used, n - 1)
                for j in range(4):
                    f = (n % 2) * 4 + j
                    last = nc.tensor.transpose(po[:, n % 2, j * P:(j + 1) * P],
                                               h[:, f, (n // 2) * P:(n // 2 + 1) * P], ident[:, :])
                last.then_inc(yt_done, 1)


_INS = ["x", "g_ffn1", "w_ffn1_gu", "w_ffn1_down", "g_mix", "w_in", "a_rel_bias", "b_sinks", "w_branch_a",
        "w_branch_b", "w_out", "g_ffn2", "w_ffn2_gu", "w_ffn2_down", "g_final"]


def kernel(**inputs):
    import numpy as np
    import concourse.bacc as bacc
    from concourse.bass_utils import run_bass_kernel_spmd as run

    half = HD // 2
    freq = np.float32(10000.0) ** (-np.arange(half, dtype=np.float32) / np.float32(half))
    angle = np.arange(S, dtype=np.float32)[None, :] * freq[:, None].astype(np.float32)
    cos, sin = np.cos(angle).astype(np.float32), np.sin(angle).astype(np.float32)
    rope = np.stack([np.concatenate([cos] * 4), np.concatenate([sin, -sin] * 2)], axis=1)

    nc = bacc.Bacc("TRN2", target_bir_lowering=False, num_devices=1)
    arrays, args = {}, []
    named = {name: np.ascontiguousarray(inputs[name]) for name in _INS}
    named["identity"] = np.eye(P, dtype=np.float32)
    named["rope"] = np.ascontiguousarray(rope)
    for name, a in named.items():
        arrays[f"in_{name}"] = a
        args.append(nc.dram_tensor(f"in_{name}", a.shape, mybir.dt.from_np(a.dtype), kind="ExternalInput").ap())
    out = nc.dram_tensor("out_y", (1, S, D), F32, kind="ExternalOutput").ap()
    build(nc, *args, out)
    r = run(nc, [arrays], core_ids=[0])
    return r.results[0]["out_y"]
```

```python
from contextlib import ExitStack

import concourse.bass as bass
from concourse import mybir

ALU = mybir.AluOpType
ACT = mybir.ActivationFunctionType
F32 = mybir.dt.float32
F32R = mybir.dt.float32r

P = 128
D = 1024
S = 512
FF = 2816
DK = D // P
FK = FF // P
QT = S // P
CH = 64
HD = 64
HEADS = 8
D_ATT = HEADS * HD
MAX_REL = 128
EPS = 1e-6
SCALE = HD ** -0.5
MASKED = -1e30 / SCALE
CW = 256
GU = FF // CW
DOWN_KB = (6, 5, 6, 5)
DOWN_K0 = (0, 6, 11, 17)
NPAIR = D // CW
EXT = S + P
FIRST_KB = 2
PARTS = 8
WARM = 11
PRODUCTS = ((0, 0), (0, 1), (1, 0))

QA0, KA0, VA0, QB0 = 0, D_ATT, 2 * D_ATT, 3 * D_ATT
KVB0 = 4 * D_ATT
GA0 = KVB0 + 4 * HD
GB0 = GA0 + D

FFN_CHUNKS = 2 * GU + NPAIR * len(DOWN_KB)
C_MIX = FFN_CHUNKS

MIX = [("qa", 0, DK), ("ka", 0, DK), ("va", 0, DK), ("va", 1, DK),
       ("qa", 1, DK), ("ka", 1, DK), ("kvb", 0, DK), ("qb", 0, DK), ("qb", 1, DK)]
for _c in range(NPAIR):
    MIX += [("ga", _c, DK), ("ya", _c, DK // 2)]
for _c in range(NPAIR):
    MIX += [("gb", _c, DK), ("yb", _c, DK // 2)]
N_TILED = len(MIX)
MIX += [("out", _c, DK) for _c in range(NPAIR)]
C_OUT = C_MIX + N_TILED
C_FFN2 = C_MIX + len(MIX)
N_CHUNKS = C_FFN2 + FFN_CHUNKS

BEFORE = [(c, m) for c in range(3) for m in range(2)]
FIRST = [(3, 0), (3, 1)]
GA, GB = MIX.index(("ga", 0, DK)), MIX.index(("gb", 0, DK))
FILL = [[(4, 0), (4, 1)], [(5, 0), (5, 1)], [(6, 0), (6, 1)], [(7, 0)], [(7, 1)], [(8, 0)], [(8, 1)]]
FILL += [[(c, 0), (c, 1)] for c in range(GA, GB)] + [[(GB, 0)]]
AFTER = [(GB, 1)] + [(c, m) for c in range(GB + 1, N_TILED) for m in range(2)]
TILES = BEFORE + FIRST + [x for f in FILL for x in f] + AFTER
X_COLS = [(0, P), (P, P)] + [(n * CW, CW) for n in range(1, NPAIR)]
LAST = [(0, 2 * P), (2 * P, 2 * P), (4 * P, 2 * P), (6 * P, P), (7 * P, P)]
NH = 2 * HEADS


def kb_of(c):
    if C_MIX <= c < C_FFN2:
        return MIX[c - C_MIX][2]
    d = c if c < C_MIX else c - C_FFN2
    return DK if d < 2 * GU else DOWN_KB[(d - 2 * GU) % len(DOWN_KB)]


def tile_kind(tau):
    c, m = TILES[tau]
    kind, i, _ = MIX[c]
    if kind == "kvb":
        kind = ("kb", "vb")[m]
    return kind, i, m


def is_partial(tau):
    return tile_kind(tau)[:2] == ("va", 0)


ROPED = [t for t in range(len(TILES)) if tile_kind(t)[0] in ("qb", "kb")]
GATES = [t for t in range(len(TILES)) if tile_kind(t)[0] in ("ga", "gb")]
SCALED = [t for t in range(len(TILES)) if tile_kind(t)[0] in ("qa", "ka")]
SPLIT = [t for t in range(len(TILES)) if tile_kind(t)[0] not in ("ga", "gb", "ya", "qb", "kb") and not is_partial(t)]
MERGED = [t for t in range(len(TILES)) if tile_kind(t)[0] == "yb"]


def plan_banks():
    banks, start, done, count, tenant = [], [], [], [0] * 6, [None] * 6
    for tau in range(len(TILES)):
        kind, i, m = tile_kind(tau)
        if kind == "va":
            own = [2 - 2 * m, 3 - 2 * m]
        elif tau < len(BEFORE):
            own = [tau] if tau < 2 else [tau + 2]
        elif tau >= len(TILES) - len(AFTER):
            own = [(tau - len(TILES)) % 4]
        else:
            own = [tau % 2]
        banks.append(own)
        start.append([] if (kind, i) == ("va", 1) else [(b, tenant[b], count[b]) for b in own])
        if not is_partial(tau):
            for b in own:
                count[b] += 1
                tenant[b] = tau
        done.append([(b, count[b]) for b in own])
    return banks, start, done


BANKS, MAY_START, READ = plan_banks()


def scratch_reader(tau):
    def slots(t):
        kind = tile_kind(t)[0]
        return {"qa": {tile_kind(t)[2]}, "ka": {tile_kind(t)[2]}, "ga": {tile_kind(t)[2]}, "gb": {tile_kind(t)[2]},
                "qb": {0, 1}, "kb": {0, 1}}.get(kind, set())
    for t in range(tau - 1, -1, -1):
        if slots(t) & slots(tau):
            if t in GATES:
                return t + 2
            return t
    return None


def splits(s):
    return [C_MIX + c + 1 for c, m in FILL[s] if m == 0]


def ropes(s):
    return [TILES.index(x) for x in FILL[s] if TILES.index(x) in ROPED]


def score_at(s, i):
    return sum(n_keys(s, j)[1] for j in range(i)) if s < HEADS else max(0, 2 * i * P - CH)


def turns(s, i):
    if s < HEADS:
        return [(j, P, j * P) for j in range(i + 1)]
    return ([(i - 1, CH, -CH)] if i else []) + [(i, P, CH if i else 0)]


def loaded_at(c):
    qb = C_MIX + MIX.index(("qb", 0, DK))
    return 32 * (c // 2 + 1) + (32 if c >= qb else 0) - (16 if c % 2 == 0 else 0)


def used_at(c):
    return c + 1 if c < C_MIX else None if c < C_OUT else c + 1 - N_TILED


def n_keys(s, i):
    first = 0 if s < HEADS else max(0, i * P - CH)
    return first, (i + 1) * P - first


def build(nc, x, g_ffn1, w_ffn1_gu, w_ffn1_down, g_mix, w_in, a_rel_bias, b_sinks, w_branch_a,
          w_branch_b, w_out, g_ffn2, w_ffn2_gu, w_ffn2_down, g_final, identity, rope, out):
    ext_dram = nc.dram_tensor("rel_bias_ext", (HEADS, EXT), F32, kind="Internal")

    ctx = ExitStack()

    def sb(stack, name, shape, dt=F32):
        return stack.enter_context(nc.sbuf_tensor(name, shape, dt))

    def psum(name, shape):
        return ctx.enter_context(nc.psum_tensor(name, shape, F32))

    def sem(name):
        return ctx.enter_context(nc.semaphore(name))

    with ctx:
        raw = sb(ctx, "raw", [P, 2, DK, CW])
        w_hl = sb(ctx, "w_hl", [P, 2, 2, DK, CW], F32R)
        early = ExitStack()
        xn = sb(early, "xn", [P, 2, DK, S], F32R)
        early.close()
        yg = sb(ctx, "yg", [P, QT, D])
        y = sb(ctx, "y", [P, QT, D])
        h = sb(ctx, "h", [P, DK, S])
        ident = sb(ctx, "ident", [P, P])
        ones = sb(ctx, "ones", [P, P])
        gains = sb(ctx, "gains", [P, 3, DK])
        eps = sb(ctx, "eps", [P, 1])
        neg = sb(ctx, "neg", [P, 2, QT])
        rows = sb(ctx, "rows", [P, 2, QT])
        esink = sb(ctx, "esink", [P, 2, QT])
        r_col = sb(ctx, "r_col", [P, QT])
        sumsq = sb(ctx, "sumsq", [P, QT, len(LAST)])
        spare = sb(ctx, "spare", [P, 1])
        r_row = sb(ctx, "r_row", [P, S])
        scr = sb(ctx, "scr", [P, 2, S])
        sinks = sb(ctx, "sinks", [P, HEADS])
        nsinks = sb(ctx, "nsinks", [P, HEADS])

        ffn = ExitStack()
        hid = sb(ffn, "hid", [P, 2, FK, S], F32R)
        silu = sb(ffn, "silu", [P, 2, S])
        work = sb(ffn, "work", [P, 2, S])
        g_fin = sb(ffn, "g_fin", [P, D])
        junk = sb(ffn, "junk", [P, 2 * P])
        ffn.close()
        begin = ExitStack()
        xin = sb(begin, "xin", [P, QT, D])
        extrow = sb(begin, "extrow", [HEADS, EXT])
        relrow = sb(begin, "relrow", [HEADS, 2 * MAX_REL + 1])
        grow = sb(begin, "grow", [3 * DK, P])
        begin.close()
        att = ExitStack()
        qa = sb(att, "qa", [P, 4, 2, S], F32R)
        qb = sb(att, "qb", [P, 4, 2, S], F32R)
        kk = sb(att, "kk", [P, 4, 2, S], F32R)
        vv = sb(att, "vv", [P, 4, 2, QT, 3, HD], F32R)
        pt = sb(att, "pt", [P, 2, QT, S], F32R)
        sc = sb(att, "sc", [P, 2, 10 * P])
        bias_a = sb(att, "bias_a", [P, S])
        cs = sb(att, "cs", [P, 2, S])
        att.close()
        mask_b = pt[:, 1, 3, 0:3 * CH].bitcast(F32)
        over = ExitStack()
        sb(over, "over_pad", [P, (3 * 8 * S + 2 * QT * 3 * HD)])
        y_gated = sb(over, "y_gated", [P, DK, S])
        over.close()

        pj = psum("pj", [P, 4, S])
        ps = psum("ps", [P, 2, S])
        po = psum("po", [P, 2, S])

        raw_in = [sem("raw_in0"), sem("raw_in1")]
        first_in = sem("first_in")
        first_hi = sem("first_hi")
        first_lo = sem("first_lo")
        hi_done = sem("hi_done")
        lo_done = sem("lo_done")
        used = sem("used")
        ident_in = sem("ident_in")
        consts_in = sem("consts_in")
        cs_in = sem("cs_in")
        x_in = [sem(f"x_in{i}") for i in range(len(X_COLS))]
        fin_in = sem("fin_in")
        ones_set = sem("ones_set")
        zeros_set = sem("zeros_set")
        mask_set = sem("mask_set")
        cs_scaled = sem("cs_scaled")
        dve = sem("dve")
        pool = sem("pool")
        gain_t = sem("gain_t")
        gain_set = sem("gain_set")
        dve_sumsq = sem("dve_sumsq")
        xt_done = sem("xt_done")
        h_set = sem("h_set")
        xn_hi = sem("xn_hi")
        xn_lo = sem("xn_lo")
        sq_pair = sem("sq_pair")
        acc_done = sem("acc_done")
        ms_done = sem("ms_done")
        rms_sqrt = sem("rms_sqrt")
        r_done = sem("r_done")
        gate_scaled = sem("gate_scaled")
        silu_done = sem("silu_done")
        gated = sem("gated")
        hid_hi = sem("hid_hi")
        hid_lo = sem("hid_lo")
        h_done = sem("h_done")
        ext_set = sem("ext_set")
        ext_out = sem("ext_out")
        bias_in = sem("bias_in")
        bias_ready = sem("bias_ready")
        tile_done = sem("tile_done")
        tile_read = [sem(f"tile_read{b}") for b in range(6)]
        scaled = sem("scaled")
        rope_swap = sem("rope_swap")
        rope_cos = sem("rope_cos")
        rope_sum = sem("rope_sum")
        split_hi = sem("split_hi")
        rot_hi = sem("rot_hi")
        gate_tanh = sem("gate_tanh")
        merged_sum = sem("merged_sum")
        merged_lo = sem("merged_lo")
        s_done = sem("s_done")
        s_used = sem("s_used")
        sink_done = sem("sink_done")
        exp_done = sem("exp_done")
        p_done = sem("p_done")
        t_done = sem("t_done")
        pt_hi = sem("pt_hi")
        pt_lo = sem("pt_lo")
        pv_done = sem("pv_done")
        o_hi = sem("o_hi")
        o_lo = sem("o_lo")
        last_down = sem("last_down")
        yt_done = sem("yt_done")
        yt_sq = sem("yt_sq")
        yt_used = sem("yt_used")
        y_done = sem("y_done")
        y_act = sem("y_act")
        out_done = sem("out_done")

        def f32(ap):
            return ap.bitcast(F32)

        def start_bank(f):
            return (ps, po)[f % 4 // 2][:, f % 2, :]

        def bank_of(tau):
            b = BANKS[tau][0]
            return ps[:, b - 4, :] if b >= 4 else pj[:, b, :]

        def turned_parts(s, i, half):
            bank = pj[:, 2 + (QT * s + i) % 2, :]
            if s < HEADS:
                return [(pt[:, half, 0:i + 1, i * P:(i + 1) * P],
                         bank[:, 0:(i + 1) * P].rearrange("p (j q) -> p j q", q=P))]
            parts, at = [], 0
            for j, nq, _ in turns(s, i):
                parts.append((pt[:, half, j, i * P:i * P + nq], bank[:, at:at + nq]))
                at += nq
            return parts

        def turned(n, i):
            _, w = LAST[n]
            return (ps if n == len(LAST) - 1 else po)[:, i // 2, (i % 2) * w:(i % 2 + 1) * w]

        def wait_used(eng, c):
            if C_MIX <= c < C_OUT:
                eng.wait_ge(tile_done, 2 * (c - C_MIX + 1))
            else:
                eng.wait_ge(used, used_at(c))

        def wait_read(eng, tau):
            for b, n in READ[tau]:
                eng.wait_ge(tile_read[b], n)

        block = ctx.enter_context(nc.Block())

        @block.sync
        def _(sp):
            def load(c, slot, halves):
                if not isinstance(c, int) or c >= 2:
                    sp.wait_ge(lo_done, c - 1)
                for dst, src in halves:
                    sp.dma_start(dst, src).then_inc(raw_in[slot], 16)

            def by_rows(slot, src, kb):
                k = kb // 2
                return [(raw[:, slot, 0:k, :], src[:, 0:k, :]), (raw[:, slot, k:kb, :], src[:, k:kb, :])]

            def load_ffn(c0, w_gu, w_down):
                gu = w_gu[0].rearrange("(k p) n -> p k n", p=P)
                down = w_down[0].rearrange("(k p) n -> p k n", p=P)
                first = 1 if c0 == 0 else 0
                with sp.Fori(first, GU) as p:
                    for j in range(2):
                        slot = (c0 + j) % 2
                        load(p * 2 + (c0 + j), slot,
                             by_rows(slot, gu[:, :, bass.ds(p * CW + j * FF, CW)], DK))
                d0 = c0 + 2 * GU
                with sp.Fori(0, NPAIR) as n:
                    for j, (k0, kb) in enumerate(zip(DOWN_K0, DOWN_KB)):
                        slot = (d0 + j) % 2
                        load(n * 4 + (d0 + j), slot,
                             by_rows(slot, down[:, k0:k0 + kb, bass.ds(n * CW, CW)], kb))

            gu1 = w_ffn1_gu[0].rearrange("(k p) n -> p k n", p=P)
            sp.dma_start(raw[:, 0, 0:FIRST_KB, :], gu1[:, 0:FIRST_KB, 0:CW]).then_inc(first_in, 16)
            sp.dma_start(ident[:, :], identity).then_inc(ident_in, 16)
            for n, g in enumerate((g_ffn1, g_mix, g_ffn2)):
                sp.dma_start(grow[n * DK:(n + 1) * DK, :], g[0].rearrange("(k p) -> k p", p=P)).then_inc(ident_in, 16)
            x_cols = x[0].rearrange("(t p) n -> p t n", p=P)
            chunk1 = by_rows(1, gu1[:, :, FF:FF + CW], DK)
            for n, (at, w) in enumerate(X_COLS):
                sp.dma_start(xin[:, :, at:at + w], x_cols[:, :, at:at + w]).then_inc(x_in[n], 16)
                if n == 2:
                    sp.dma_start(raw[:, 0, FIRST_KB:DK, :], gu1[:, FIRST_KB:DK, 0:CW]).then_inc(raw_in[0], 16)
            for half in chunk1:
                sp.dma_start(*half).then_inc(raw_in[1], 16)
            load_ffn(0, w_ffn1_gu, w_ffn1_down)

            win = w_in[0].rearrange("(k p) n -> p k n", p=P)
            wa = w_branch_a[0].rearrange("(k p) n -> p k n", p=P)
            wb = w_branch_b[0].rearrange("(g t p) n -> g p t n", g=2, t=4)
            wo = w_out[0].rearrange("(k p) n -> p k n", p=P)
            col0 = {"qa": QA0, "ka": KA0, "kvb": KVB0, "ga": GA0, "gb": GB0}
            for n, (kind, i, kb) in enumerate(MIX):
                c = C_MIX + n
                slot = c % 2
                cols = slice(i * CW, (i + 1) * CW)
                if kind == "qb":
                    halves = []
                    for j in range(2):
                        for g in range(2):
                            c1 = QB0 + (2 * i + j + 4 * g) * HD
                            halves.append((raw[:, slot, :, (2 * j + g) * HD:(2 * j + g + 1) * HD],
                                           win[:, :, c1:c1 + HD]))
                elif kind == "va":
                    rows_of = win[:, 4 * i:4 * i + 4, VA0:VA0 + 2 * CW]
                    wide = raw[:, slot, :, :].rearrange("p (k two) n -> p k (two n)", two=2)
                    halves = [(wide[:, 0:2, :], rows_of[:, 0:2, :]), (wide[:, 2:4, :], rows_of[:, 2:4, :])]
                elif kind == "ya":
                    halves = by_rows(slot, wa[:, :, cols], kb)
                elif kind == "yb":
                    halves = [(raw[g * HD:(g + 1) * HD, slot, 0:kb, :], wb[g][:, :, cols]) for g in range(2)]
                elif kind == "out":
                    halves = by_rows(slot, wo[:, :, cols], kb)
                else:
                    c1 = col0[kind] + i * CW
                    halves = by_rows(slot, win[:, :, c1:c1 + CW], kb)
                load(c, slot, halves)
            load_ffn(C_FFN2, w_ffn2_gu, w_ffn2_down)
            for i in range(QT):
                sp.wait_ge(y_act if i % 2 else y_done, i // 2 + 1)
                sp.dma_start(out[0, i * P:(i + 1) * P, :], y[:, i, :]).then_inc(out_done, 16)
            sp.wait_ge(out_done, 16 * QT)

        @block.gpsimd
        def _(pl):
            pl.memset(ones[:, :], 1.0).then_inc(ones_set, 1)
            pl.memset(eps[:, :], EPS).then_inc(ones_set, 1)
            pl.dma_start(relrow[:, :], a_rel_bias[0]).then_inc(consts_in, 16)
            pl.dma_start(sinks[:, :], b_sinks[0].partition_broadcast(P)).then_inc(consts_in, 16)
            pl.wait_ge(ext_set, 2)
            pl.dma_start(ext_dram[:, :], extrow[:, :]).then_inc(ext_out, 16)
            pl.wait_ge(ext_out, 16)
            pl.wait_ge(r_done, 3)
            pl.memset(f32(vv[:, :, :, :, 1, :]).rearrange("p a b c d -> p (a b c) d"), 0.0).then_inc(zeros_set, 1)

            def split(c, slot, kb):
                pl.wait_ge(lo_done, c)
                pl.wait_ge(hi_done, c + 1)
                nc.gpsimd.tensor_tensor(w_hl[:, slot, 1, 0:kb, :], raw[:, slot, 0:kb, :],
                                        f32(w_hl[:, slot, 0, 0:kb, :]), ALU.subtract).then_inc(lo_done, 1)

            pl.dma_start(cs[:, :, :], rope).then_inc(cs_in, 16)
            pl.wait_ge(cs_in, 16)
            for j in range(2):
                nc.gpsimd.tensor_tensor(cs[:, j, :], cs[:, j, :], r_row[:, :], ALU.mult).then_inc(cs_scaled, 1)

            def rotate(n):
                pl.wait_ge(rope_swap, n + 1)
                if n == 0:
                    pl.wait_ge(cs_scaled, 2)
                nc.gpsimd.tensor_tensor(scr[:, 1, :], scr[:, 1, :], cs[:, 1, :], ALU.mult).then_inc(pool, 1)
                pl.wait_ge(pool, n + 1)
                pl.wait_ge(rope_cos, n + 1)
                nc.gpsimd.tensor_tensor(scr[:, 0, :], scr[:, 0, :], scr[:, 1, :], ALU.add).then_inc(rope_sum, 1)

            pl.memset(mask_b, 0.0).then_inc(mask_set, 1)
            pl.wait_ge(mask_set, 1)
            pl.memset(mask_b[0:CH, 2 * CH:3 * CH], MASKED).then_inc(mask_set, 1)
            pl.memset(mask_b[CH:P, 0:CH], MASKED).then_inc(mask_set, 1)
            pl.wait_ge(mask_set, 3)
            n = 0
            for s in range(NH):
                for c in splits(s):
                    split(c, c % 2, kb_of(c))
                for _tile in ropes(s):
                    rotate(n)
                    n += 1
            pl.wait_ge(acc_done, 3 * NPAIR)
            pl.dma_start(g_fin[:, :], g_final.partition_broadcast(P)).then_inc(fin_in, 16)

        @block.scalar
        def _(act):
            def split(c, slot, kb):
                act.wait_ge(raw_in[slot], loaded_at(c))
                if c >= 2:
                    wait_used(act, c - 2)
                nc.scalar.activation(w_hl[:, slot, 0, 0:kb, :], raw[:, slot, 0:kb, :],
                                     ACT.Copy).then_inc(hi_done, 1)

            def split_at(c_of, reg, slot, kb):
                per, base = c_of
                act.wait_ge(raw_in[slot], reg * (16 * per) + loaded_at(base))
                act.wait_ge(used, reg * per + used_at(base - 2))
                nc.scalar.activation(w_hl[:, slot, 0, 0:kb, :], raw[:, slot, 0:kb, :],
                                     ACT.Copy).then_inc(hi_done, 1)

            def copy_hi(dst, src):
                return nc.scalar.activation(dst, src, ACT.Copy)

            def prepare(n, k):
                act.wait_ge(h_done, DK * (n - 1) + k + 1)
                nc.scalar.activation(xn[:, 0, k, :], h[:, k, :], ACT.Copy,
                                     scale=gains[:, n, k:k + 1]).then_inc(xn_hi, 1)

            def squares(n, pair):
                if n or pair:
                    act.wait_ge(acc_done, NPAIR * n + pair)
                nc.scalar.activation(silu[:, :, :], h[:, 2 * pair:2 * pair + 2, :], ACT.Square).then_inc(sq_pair, 1)

            def preload(func):
                nc.scalar.activation(spare[:, :], eps[:, :], func)

            def root(n):
                preload(ACT.Sqrt)
                act.wait_ge(ms_done, n + 1)
                nc.scalar.activation(r_row[:, :], po[:, 0, :], ACT.Sqrt, bias=eps[:, :],
                                     scale=1.0 / D).then_inc(rms_sqrt, 1)
                if n == 1:
                    nc.scalar.activation(r_col[:, :], po[:, 1, 0:QT], ACT.Sqrt, bias=eps[:, :],
                                         scale=1.0 / D).then_inc(rms_sqrt, 1)

            act.wait_ge(first_in, 16)
            copy_hi(w_hl[:, 0, 0, 0:FIRST_KB, :], raw[:, 0, 0:FIRST_KB, :]).then_inc(first_hi, 1)
            act.wait_ge(gain_set, 1)
            for f in range(DK):
                act.wait_ge(xt_done, f + 1)
                nc.scalar.activation(xn[:, 0, f, :], start_bank(f), ACT.Copy,
                                     scale=gains[:, 0, f:f + 1]).then_inc(xn_hi, 1)
                copy_hi(h[:, f, :], start_bank(f)).then_inc(h_set, 1)
                if f == 1:
                    act.wait_ge(raw_in[0], loaded_at(0))
                    copy_hi(w_hl[:, 0, 0, FIRST_KB:DK, :], raw[:, 0, FIRST_KB:DK, :]).then_inc(hi_done, 1)
                elif f == 3:
                    act.wait_ge(h_set, 4)
                    squares(0, 0)
                elif f == 5:
                    split(1, 1, DK)
            act.wait_ge(ones_set, 2)
            act.wait_ge(h_set, DK)
            for pair in range(1, NPAIR):
                squares(0, pair)

            def ffn_act(c0, f):
                def gate(p):
                    act.wait_ge(gate_scaled, p + (f * GU + 1))
                    nc.scalar.activation(silu[:, :, :], silu[:, :, :], ACT.Silu).then_inc(silu_done, 1)

                def hidden(p):
                    act.wait_ge(gated, p + (f * GU + 1))
                    nc.scalar.activation(hid[:, 0, bass.ds(p * 2, 2), :], work[:, :, :],
                                         ACT.Copy).then_inc(hid_hi, 1)

                split(c0 + 2, c0 % 2, DK)
                root(2 * f)
                split(c0 + 3, (c0 + 1) % 2, DK)
                gate(0)
                hidden(0)
                gate(1)
                with act.Fori(1, GU - 1) as p:
                    split_at((2, c0 + 2), p, c0 % 2, DK)
                    hidden(p)
                    split_at((2, c0 + 3), p, (c0 + 1) % 2, DK)
                    gate(p + 1)
                d0 = c0 + 2 * GU
                split(d0, d0 % 2, DOWN_KB[0])
                hidden(GU - 1)
                for n in range(NPAIR):
                    for j in range(1, 5):
                        c = d0 + 4 * n + j
                        if c < N_CHUNKS:
                            split(c, c % 2, kb_of(c))
                    if f == 0:
                        prepare(1, 2 * n)
                        prepare(1, 2 * n + 1)
                        squares(1, n)
                    elif n:
                        last_squares(n - 1)

            def last_squares(n):
                _, w = LAST[n]
                slots = 2 * P // w
                act.wait_ge(yt_done, n + 1)
                for j, i in enumerate((2, 3, 0, 1)):
                    before = QT * n + j - (slots - 1)
                    if slots == 2:
                        before = max(before, QT * (len(LAST) - 2))
                    if before:
                        act.wait_ge(yt_sq, before)
                    if j == 2:
                        act.wait_ge(yt_used, 2 * n + 1)
                    nc.scalar.activation(junk[:, j % slots * w:(j % slots + 1) * w], turned(n, i), ACT.Square,
                                         accum_out=sumsq[:, i, n:n + 1]).then_inc(yt_sq, 1)

            ffn_act(0, 0)

            def start_chunk(c):
                c += C_MIX + 1
                split(c, c % 2, kb_of(c))

            def evacuate(tau):
                kind, i, m = tile_kind(tau)
                if is_partial(tau):
                    return
                bank = bank_of(tau)
                t = 2 * i + m
                if kind in ("qa", "ka"):
                    act.wait_ge(scaled, SCALED.index(tau) + 1)
                    copy_hi((qa if kind == "qa" else kk)[:, t, 0, :], scr[:, m, :]).then_inc(split_hi, 1)
                elif kind == "va":
                    act.wait_ge(tile_done, tau + 1)
                    act.wait_ge(r_done, 3)
                    for j in BANKS[tau]:
                        last = nc.scalar.activation(vv[:, :, 0, j, 0:3:2, :],
                                                    pj[:, j, :].rearrange("p (a b d) -> p a b d", a=4, b=2),
                                                    ACT.Copy, scale=r_col[:, j:j + 1])
                    last.then_inc(split_hi, 1)
                elif kind == "vb":
                    act.wait_ge(tile_done, tau + 1)
                    for j in range(QT):
                        last = nc.scalar.activation(vv[:, 0, 0, j, 0:3:2, :],
                                                    bank[:, j * P:(j + 1) * P].rearrange("p (b d) -> p b d", b=2),
                                                    ACT.Copy, scale=r_col[:, j:j + 1])
                    last.then_inc(split_hi, 1)
                elif kind in ("qb", "kb"):
                    act.wait_ge(rope_cos, ROPED.index(tau) + 1)
                    for q in range(4):
                        o = q ^ 1
                        last = copy_hi(scr[32 * q:32 * q + 32, 1, :], bank[32 * o:32 * o + 32, :])
                    last.then_inc(rope_swap, 1)
                elif kind in ("ga", "gb"):
                    wait_read(act, tau)
                    nc.scalar.activation(scr[:, m, :], scr[:, m, :], ACT.Tanh, scale=0.5).then_inc(gate_tanh, 1)
                elif kind == "yb":
                    n = MERGED.index(tau)
                    act.wait_ge(merged_sum, n + 1)
                    copy_hi(qa[:, t // 2, t % 2, :], sc[:, n % 2, 0:S]).then_inc(split_hi, 1)

            def rotated_hi(tau):
                kind, i, m = tile_kind(tau)
                act.wait_ge(rope_sum, ROPED.index(tau) + 1)
                copy_hi(qb[:, 2 * i + m, 0, :] if kind == "qb" else kk[:, 0, 0, :], scr[:, 0, :]).then_inc(rot_hi, 1)

            def exponentials(s, i, at):
                _, n = n_keys(s, i)
                act.wait_ge(s_used, QT * s + i + 1)
                e = sc[:, s % 2, at:at + n]
                nc.scalar.activation(e, e, ACT.Exp, bias=neg[:, s % 2, i:i + 1], scale=-1.0,
                                     accum_out=rows[:, s % 2, i:i + 1]).then_inc(exp_done, 1)
                if s >= HEADS and i == QT - 1:
                    hq = (s - HEADS) // 2 + 4 * (s % 2)
                    nc.scalar.activation(esink[:, s % 2, :], neg[:, s % 2, :], ACT.Exp,
                                         bias=sinks[:, hq:hq + 1]).then_inc(sink_done, 1)

            def turned_hi(s, i):
                u = QT * s + i
                act.wait_ge(t_done, u + 1)
                if s:
                    act.wait_ge(pv_done, s)
                for dst, src in turned_parts(s, i, 0):
                    last = copy_hi(dst, src)
                last.then_inc(pt_hi, 1)

            def load_bias(s):
                if s:
                    act.wait_ge(s_used, QT * s)
                else:
                    act.wait_ge(ext_out, 16)
                    act.wait_ge(r_done, 3)
                src = bass.AP(ext_dram, s * EXT, [[1, P], [1, S]])
                act.dma_start(bias_a[:, :], src).then_inc(bias_in, 16)

            def output_hi(pr):
                act.wait_ge(pv_done, 2 * pr + 2)
                copy_hi((qa if pr < 4 else qb)[:, pr % 4, 0, :], po[:, pr % 2, :]).then_inc(o_hi, 1)

            tau = 0
            for c, m in BEFORE:
                if m == 0:
                    start_chunk(c)
                if tau == 0:
                    root(1)
                if tau == 2:
                    load_bias(0)
                    evacuate(0)
                    evacuate(1)
                if tau >= 2:
                    evacuate(tau)
                tau += 1
            for i in range(QT):
                exponentials(0, i, score_at(0, i))
            load_bias(1)
            for c, m in FIRST:
                if m == 0:
                    start_chunk(c)
                    evacuate(tau)
                tau += 1

            for s in range(NH):
                for i in range(QT):
                    turned_hi(s, i)
                    if s + 1 < NH:
                        exponentials(s + 1, i, score_at(s + 1, i))
                    if s == 0 and i == 1:
                        evacuate(tau - 1)
                    if s and i == 1:
                        if s % 2 == 0:
                            output_hi(s // 2 - 1)
                        for x in ropes(s - 1):
                            rotated_hi(x)
                    if i == 1:
                        for c in splits(s):
                            split(c, c % 2, kb_of(c))
                if s + 2 < HEADS:
                    load_bias(s + 2)
                for _tile in FILL[s]:
                    evacuate(tau)
                    tau += 1
            output_hi(NH // 2 - 1)
            for c, m in AFTER:
                if m == 1:
                    start_chunk(c + 1)
                evacuate(tau)
                tau += 1
            for n in range(NPAIR):
                c = C_OUT + n + 2
                prepare(2, 2 * n)
                prepare(2, 2 * n + 1)
                squares(2, n)
                split(c, c % 2, kb_of(c))
            ffn_act(C_FFN2, 1)

            preload(ACT.Sqrt)
            last_squares(len(LAST) - 2)
            last_squares(len(LAST) - 1)
            act.wait_ge(dve_sumsq, 1)
            nc.scalar.activation(neg[:, 0, :], rows[:, 0, :], ACT.Sqrt, bias=eps[:, :],
                                 scale=1.0 / D).then_inc(rms_sqrt, 1)
            act.wait_ge(r_done, 5)
            for i in range(1, QT, 2):
                nc.scalar.activation(y[:, i, :], yg[:, i, :], ACT.Copy, scale=r_col[:, i:i + 1]).then_inc(y_act, 1)

        @block.vector
        def _(ve):
            own = [0]

            def link(ins):
                own[0] += 1
                ins.then_inc(dve, 1)
                ve.wait_ge(dve, own[0])

            def minus_hi(dst, src, hi):
                return nc.vector.tensor_tensor(dst, src, f32(hi), ALU.subtract)

            def split(c, slot, kb):
                ve.wait_ge(hi_done, c + 1)
                minus_hi(w_hl[:, slot, 1, 0:kb, :], raw[:, slot, 0:kb, :],
                         w_hl[:, slot, 0, 0:kb, :]).then_inc(lo_done, 1)

            def prepare(n, k, src):
                ve.wait_ge(xn_hi, DK * n + k + 1)
                nc.vector.scalar_tensor_tensor(xn[:, 1, k, :], src, gains[:, n, k:k + 1], f32(xn[:, 0, k, :]),
                                               ALU.mult, ALU.subtract).then_inc(xn_lo, 1)

            def sums(n, pair):
                ve.wait_ge(sq_pair, NPAIR * n + pair + 1)
                if pair == 0:
                    nc.vector.tensor_tensor(scr[:, 0, :], silu[:, 0, :], silu[:, 1, :], ALU.add).then_inc(acc_done, 1)
                else:
                    link(nc.vector.tensor_tensor(scr[:, 0, :], scr[:, 0, :], silu[:, 0, :], ALU.add))
                    nc.vector.tensor_tensor(scr[:, 0, :], scr[:, 0, :], silu[:, 1, :], ALU.add).then_inc(acc_done, 1)
                ve.wait_ge(acc_done, NPAIR * n + pair + 1)

            def inverse(n):
                ve.wait_ge(rms_sqrt, n + 1 + (n == 2))
                nc.vector.reciprocal(r_row[:, :], r_row[:, :]).then_inc(r_done, 1)
                if n == 1:
                    ve.wait_ge(rms_sqrt, 3)
                    nc.vector.reciprocal(r_col[:, :], r_col[:, :]).then_inc(r_done, 1)
                ve.wait_ge(r_done, (1, 3, 4)[n])

            ve.wait_ge(gain_t, 1)
            nc.vector.tensor_copy(gains[:, :, :].rearrange("p n k -> p (n k)"),
                                  pj[:, 3, 0:3 * DK]).then_inc(gain_set, 1)
            ve.wait_ge(gain_set, 1)
            ve.wait_ge(first_hi, 1)
            minus_hi(w_hl[:, 0, 1, 0:FIRST_KB, :], raw[:, 0, 0:FIRST_KB, :],
                     w_hl[:, 0, 0, 0:FIRST_KB, :]).then_inc(first_lo, 1)
            for f in range(DK):
                ve.wait_ge(h_set, f + 1)
                prepare(0, f, h[:, f, :])
                if f == 1:
                    ve.wait_ge(hi_done, 1)
                    minus_hi(w_hl[:, 0, 1, FIRST_KB:DK, :], raw[:, 0, FIRST_KB:DK, :],
                             w_hl[:, 0, 0, FIRST_KB:DK, :]).then_inc(lo_done, 1)
                elif f == 4:
                    sums(0, 0)
                elif f == 5:
                    split(1, 1, DK)
            for pair in range(1, NPAIR):
                sums(0, pair)

            def bias_rows():
                ve.wait_ge(consts_in, 16 * 2)
                link(nc.vector.tensor_scalar(nsinks[:, :], sinks[:, :], -1.0, None, ALU.mult))
                near = P + MAX_REL - 1
                nc.vector.tensor_scalar(extrow[:, 0:near], relrow[:, 1:near + 1], 1.0 / SCALE, None,
                                        ALU.mult).then_inc(ext_set, 1)
                link(nc.vector.memset(extrow[:, near:EXT], 1.0 / SCALE))
                nc.vector.tensor_scalar(extrow[:, near:EXT], extrow[:, near:EXT],
                                        relrow[:, 2 * MAX_REL:2 * MAX_REL + 1], None, ALU.mult).then_inc(ext_set, 1)

            def ffn_dve(c0, f):
                def scale_gate(p, banks=pj):
                    if not isinstance(p, int) or p:
                        ve.wait_ge(gated, p + f * GU)
                    ve.wait_ge(used, p * 2 + used_at(c0))
                    for m in range(2):
                        last = nc.vector.tensor_tensor(silu[:, m, :], banks[:, m, :], r_row[:, :], ALU.mult)
                    last.then_inc(gate_scaled, 1)

                def product(p):
                    ve.wait_ge(silu_done, p + (f * GU + 1))
                    ve.wait_ge(used, p * 2 + used_at(c0 + 1))
                    nc.vector.tensor_tensor(work[:, :, :], silu[:, :, :], pj[:, 2:4, :],
                                            ALU.mult).then_inc(gated, 1)

                def hidden_lo(p):
                    ve.wait_ge(hid_hi, p + (f * GU + 1))
                    minus_hi(hid[:, 1, bass.ds(p * 2, 2), :], work[:, :, :],
                             hid[:, 0, bass.ds(p * 2, 2), :]).then_inc(hid_lo, 1)

                split(c0 + 2, c0 % 2, DK)
                if f == 0:
                    bias_rows()
                inverse(2 * f)
                scale_gate(0)
                split(c0 + 3, (c0 + 1) % 2, DK)
                if f == 0:
                    ve.wait_ge(ext_out, 16)
                product(0)
                hidden_lo(0)
                scale_gate(1, ps)
                with ve.Fori(1, GU - 1) as p:
                    split(p * 2 + (c0 + 2), c0 % 2, DK)
                    product(p)
                    hidden_lo(p)
                    split(p * 2 + (c0 + 3), (c0 + 1) % 2, DK)
                    scale_gate(p + 1)
                d0 = c0 + 2 * GU
                split(d0, d0 % 2, DOWN_KB[0])
                product(GU - 1)
                hidden_lo(GU - 1)
                ve.wait_ge(hid_lo, (f + 1) * GU)

                def add(n):
                    final = d0 + 4 * n + 3 == N_CHUNKS - 1
                    if not final:
                        ve.wait_ge(used, used_at(d0 + 4 * n + 3))
                    for m in range(2):
                        k = 2 * n + m
                        if final and m == 1:
                            times_gain(len(LAST) - 2)
                        if final:
                            ve.wait_ge(last_down, m + 1)
                        link(nc.vector.scalar_tensor_tensor(work[:, m, :], pj[:, 2 * (n % 2) + m, :], 0.5,
                                                            r_row[:, :], ALU.mult, ALU.mult))
                        nc.vector.tensor_tensor(h[:, k, :], h[:, k, :], work[:, m, :], ALU.add).then_inc(h_done, 1)
                    ve.wait_ge(h_done, 2 * DK * f + 2 * n + 2)

                for n in range(NPAIR):
                    for j in range(1, 5):
                        c = d0 + 4 * n + j
                        if c < N_CHUNKS:
                            split(c, c % 2, kb_of(c))
                    if f and n:
                        times_gain(n - 1)
                    add(n)
                    if f == 0:
                        prepare(1, 2 * n, h[:, 2 * n, :])
                        prepare(1, 2 * n + 1, h[:, 2 * n + 1, :])
                        sums(1, n)

            def times_gain(n):
                at, w = LAST[n]
                ve.wait_ge(yt_done, n + 1)
                ve.wait_ge(fin_in, 16)
                for i in range(QT):
                    if i == 2:
                        ve.wait_ge(yt_sq, QT * n + 2)
                    last = nc.vector.tensor_tensor(yg[:, i, at:at + w], turned(n, i), g_fin[:, at:at + w], ALU.mult)
                    if i % 2:
                        last.then_inc(yt_used, 1)

            ffn_dve(0, 0)

            def start_chunk(c):
                c += C_MIX + 1
                split(c, c % 2, kb_of(c))

            def evacuate(tau):
                kind, i, m = tile_kind(tau)
                if is_partial(tau):
                    return
                bank = bank_of(tau)
                read = tile_read[BANKS[tau][-1]]
                t = 2 * i + m
                if kind in ("qa", "ka", "ga", "gb"):
                    if (before := scratch_reader(tau)) is not None:
                        wait_read(ve, before)
                    ve.wait_ge(tile_done, tau + 1)
                    nc.vector.tensor_tensor(scr[:, m, :], bank, r_row[:, :],
                                            ALU.mult).then_inc(scaled if kind in ("qa", "ka") else read, 1)
                if kind in ("qa", "ka"):
                    dst = qa if kind == "qa" else kk
                    ve.wait_ge(split_hi, SPLIT.index(tau) + 1)
                    minus_hi(dst[:, t, 1, :], scr[:, m, :], dst[:, t, 0, :]).then_inc(read, 1)
                elif kind == "va":
                    ve.wait_ge(split_hi, SPLIT.index(tau) + 1)
                    for j in BANKS[tau]:
                        src = pj[:, j, :].rearrange("p (a b d) -> p a b d", a=4, b=2)
                        for b in range(2):
                            last = nc.vector.scalar_tensor_tensor(
                                vv[:, :, 1, j, 2 * b, :], src[:, :, b, :], r_col[:, j:j + 1],
                                f32(vv[:, :, 0, j, 2 * b, :]), ALU.mult, ALU.subtract)
                        last.then_inc(tile_read[j], 1)
                elif kind == "vb":
                    ve.wait_ge(split_hi, SPLIT.index(tau) + 1)
                    for j in range(QT):
                        last = nc.vector.scalar_tensor_tensor(
                            vv[:, 0, 1, j, 0:3:2, :], bank[:, j * P:(j + 1) * P].rearrange("p (b d) -> p b d", b=2),
                            r_col[:, j:j + 1], f32(vv[:, 0, 0, j, 0:3:2, :]), ALU.mult, ALU.subtract)
                    last.then_inc(read, 1)
                elif kind in ("qb", "kb"):
                    n = ROPED.index(tau)
                    ve.wait_ge(cs_scaled, 2)
                    ve.wait_ge(tile_done, tau + 1)
                    nc.vector.tensor_tensor(scr[:, 0, :], bank, cs[:, 0, :], ALU.mult).then_inc(rope_cos, 1)
                elif kind == "ya":
                    ve.wait_ge(gate_tanh, GATES.index(tau - 2) + 1)
                    ve.wait_ge(tile_done, tau + 1)
                    nc.vector.scalar_tensor_tensor(y_gated[:, t, :], scr[:, m, :], 1.0, bank, ALU.add,
                                                   ALU.mult).then_inc(read, 1)
                elif kind == "yb":
                    n = MERGED.index(tau)
                    if n >= 2:
                        ve.wait_ge(merged_lo, n - 1)
                    ve.wait_ge(gate_tanh, GATES.index(tau - 2) + 1)
                    ve.wait_ge(tile_done, tau + 1)
                    merged = sc[:, n % 2, 0:S]
                    nc.vector.scalar_tensor_tensor(merged, scr[:, m, :], 1.0, bank, ALU.add,
                                                   ALU.mult).then_inc(read, 1)
                    wait_read(ve, tau)
                    nc.vector.tensor_tensor(merged, merged, y_gated[:, t, :], ALU.add).then_inc(merged_sum, 1)
                    ve.wait_ge(split_hi, SPLIT.index(tau) + 1)
                    minus_hi(pt[:, t // 4, t % 4, :], merged, qa[:, t // 2, t % 2, :]).then_inc(merged_lo, 1)

            def rotated_lo(tau):
                kind, i, m = tile_kind(tau)
                dst = qb[:, 2 * i + m, :, :] if kind == "qb" else kk[:, 0, :, :]
                ve.wait_ge(rot_hi, ROPED.index(tau) + 1)
                minus_hi(dst[:, 1, :], scr[:, 0, :], dst[:, 0, :]).then_inc(tile_read[BANKS[tau][0]], 1)

            def scored(s, i):
                b = s >= HEADS
                hq = (s - HEADS) // 2 + 4 * (s % 2)
                u = QT * s + i
                _, n = n_keys(s, i)
                at = score_at(s, i)
                if i == 0:
                    if s == HEADS:
                        ve.wait_ge(mask_set, 3)
                    if s >= 2:
                        ve.wait_ge(t_done, QT * (s - 1))
                    if s in (HEADS, HEADS + 1):
                        wide = sc[:, s % 2, P:P + 2 * P * (QT - 1)].rearrange("p (i w) -> p i w", w=2 * P)
                        nc.vector.memset(wide[:, :, 0:CH], 0.0)
                ve.wait_ge(s_done, u + 1)
                table = mask_b[:, 3 * CH - n:3 * CH] if b else bias_a[:, n - 1::-1]
                lowest = nsinks[:, hq:hq + 1] if b else -MASKED
                nc.vector.tensor_tensor_reduce(sc[:, s % 2, at:at + n], ps[:, u % 2, 0:n], table, -SCALE, lowest,
                                               ALU.add, ALU.min, neg[:, s % 2, i:i + 1]).then_inc(s_used, 1)

            def mask_bias(s):
                ve.wait_ge(bias_in, 16 * (s + 1))
                nc.vector.memset(bias_a[0:CH, 0:CH], MASKED).then_inc(bias_ready, 1)
                ve.wait_ge(bias_ready, s + 1)

            def probabilities(s):
                r = rows[:, s % 2, :]
                ve.wait_ge(exp_done, QT * (s + 1))
                if s >= HEADS:
                    ve.wait_ge(sink_done, s - HEADS + 1)
                    link(nc.vector.tensor_tensor(r, r, esink[:, s % 2, :], ALU.add))
                link(nc.vector.reciprocal(r, r))
                for i in range(QT):
                    _, n = n_keys(s, i)
                    e = sc[:, s % 2, score_at(s, i):score_at(s, i) + n]
                    nc.vector.tensor_scalar(e, e, rows[:, s % 2, i:i + 1], None, ALU.mult).then_inc(p_done, 1)

            def turned_lo(s, i):
                ve.wait_ge(pt_hi, QT * s + i + 1)
                for (dst, src), (hi, _) in zip(turned_parts(s, i, 1), turned_parts(s, i, 0)):
                    last = minus_hi(dst, src, hi)
                last.then_inc(pt_lo, 1)

            def output_lo(pr):
                dst = qa if pr < 4 else qb
                ve.wait_ge(o_hi, pr + 1)
                minus_hi(dst[:, pr % 4, 1, :], po[:, pr % 2, :], dst[:, pr % 4, 0, :]).then_inc(o_lo, 1)

            tau = 0
            for c, m in BEFORE:
                if m == 0:
                    start_chunk(c)
                if tau == 0:
                    inverse(1)
                if tau == 2:
                    evacuate(0)
                    evacuate(1)
                if tau >= 2:
                    evacuate(tau)
                tau += 1
            mask_bias(0)
            for i in range(QT):
                scored(0, i)
            probabilities(0)
            for c, m in FIRST:
                if m == 0:
                    start_chunk(c)
                    evacuate(tau)
                tau += 1
            mask_bias(1)
            for s in range(NH):
                for i in range(QT):
                    if s + 1 < NH:
                        scored(s + 1, i)
                    turned_lo(s, i)
                    if s == 0 and i == 1:
                        evacuate(tau - 1)
                    if s and i == 1:
                        if s % 2 == 0:
                            output_lo(s // 2 - 1)
                        for x in ropes(s - 1):
                            rotated_lo(x)
                alone = len(FILL[s]) == 1 and bool(ropes(s))
                if alone:
                    evacuate(tau)
                if s + 1 < NH:
                    probabilities(s + 1)
                if not alone:
                    for n in range(len(FILL[s])):
                        evacuate(tau + n)
                tau += len(FILL[s])
                if s + 2 < HEADS:
                    mask_bias(s + 2)
            output_lo(NH // 2 - 1)
            ve.wait_ge(lo_done, C_MIX + AFTER[0][0] + 2)
            for c, m in AFTER:
                if m == 1:
                    start_chunk(c + 1)
                evacuate(tau)
                tau += 1
            for n in range(NPAIR):
                c = C_OUT + n + 2
                wait_used(ve, C_OUT + n)
                for m in range(2):
                    k = 2 * n + m
                    nc.vector.scalar_tensor_tensor(h[:, k, :], pj[:, 2 * (n % 2) + m, :], 0.5, h[:, k, :], ALU.mult,
                                                   ALU.add).then_inc(h_done, 1)
                ve.wait_ge(h_done, DK + 2 * n + 2)
                prepare(2, 2 * n, h[:, 2 * n, :])
                prepare(2, 2 * n + 1, h[:, 2 * n + 1, :])
                sums(2, n)
                split(c, c % 2, kb_of(c))
            ffn_dve(C_FFN2, 1)

            times_gain(len(LAST) - 1)
            ve.wait_ge(yt_sq, QT * len(LAST))
            nc.vector.tensor_reduce(rows[:, 0, :], sumsq[:, :, :], mybir.AxisListType.X, ALU.add).then_inc(dve_sumsq, 1)
            ve.wait_ge(rms_sqrt, 5)
            nc.vector.reciprocal(r_col[:, :], neg[:, 0, :]).then_inc(r_done, 1)
            ve.wait_ge(r_done, 5)
            for i in range(0, QT, 2):
                nc.vector.tensor_scalar(y[:, i, :], yg[:, i, :], r_col[:, i:i + 1], None, ALU.mult).then_inc(y_done, 1)

        @block.tensor
        def _(pe):
            def project(out_banks, slot, kb, moving, start=True, stop=True, ready=None):
                for k in range(kb):
                    if ready:
                        ready(k)
                    for m in range(2):
                        for wh, xh in PRODUCTS:
                            last = nc.tensor.matmul(out_banks[:, m, :], w_hl[:, slot, wh, k, m * P:(m + 1) * P],
                                                    moving(xh, k), start=start and k == 0 and (wh, xh) == (0, 0),
                                                    stop=stop and k == kb - 1 and (wh, xh) == PRODUCTS[-1])
                return last

            def of_xn(xh, k):
                return xn[:, xh, k, :]

            pe.wait_ge(ones_set, 1)
            for _n in range(WARM):
                nc.tensor.matmul(po[:, 1, 0:P], ones[:, :], ones[:, :], start=True, stop=True)

            pe.wait_ge(ident_in, 64)
            nc.tensor.transpose(pj[:, 3, 0:3 * DK], grow[:, :], ident[0:3 * DK, 0:3 * DK]).then_inc(gain_t, 1)

            def turn_x(f):
                if f < 2:
                    pe.wait_ge(x_in[f], 16)
                elif f % 2 == 0:
                    pe.wait_ge(x_in[f // 2 + 1], 16)
                if f >= 4:
                    pe.wait_ge(h_set, f - 3)
                for i in range(QT):
                    last = nc.tensor.transpose(start_bank(f)[:, i * P:(i + 1) * P], xin[:, i, f * P:(f + 1) * P],
                                               ident[:, :])
                last.then_inc(xt_done, 1)

            for f in range(4):
                turn_x(f)

            def ffn_pe(c0, f, xn_ready):
                def gate(p, ready=None, banks=pj[:, 0:2, :]):
                    if not isinstance(p, int) or p or f:
                        pe.wait_ge(lo_done, p * 2 + (c0 + 1))
                    if not isinstance(p, int):
                        pe.wait_ge(gate_scaled, p + f * GU)
                    project(banks, c0 % 2, DK, of_xn, ready=ready).then_inc(used, 1)

                def up(p, ready=None):
                    pe.wait_ge(lo_done, p * 2 + (c0 + 2))
                    if not isinstance(p, int) or p:
                        pe.wait_ge(gated, p + f * GU)
                    project(pj[:, 2:4, :], (c0 + 1) % 2, DK, of_xn, ready=ready).then_inc(used, 1)

                gate(0, xn_ready)
                up(0, lambda k: mean_square(2 * f) if k == (0 if f else DK // 2) else None)
                gate(1, banks=ps[:, 0:2, :])
                up(1)
                with pe.Fori(2, GU) as p:
                    gate(p)
                    up(p)
                d0 = c0 + 2 * GU
                for n in range(NPAIR):
                    pair = 2 * (n % 2)
                    for j, (k0, kb) in enumerate(zip(DOWN_K0, DOWN_KB)):
                        c = d0 + 4 * n + j
                        pe.wait_ge(lo_done, c + 1)
                        if n == 0 and j == 0:
                            pe.wait_ge(gate_scaled, (f + 1) * GU)
                        if n == 0 and j == 3:
                            pe.wait_ge(hid_lo, (f + 1) * GU)
                        elif n == 0:
                            pe.wait_ge(hid_lo, f * GU + (k0 + kb + 1) // 2)
                        if j == 0 and n == 1:
                            pe.wait_ge(gated, (f + 1) * GU)
                        if j == 0 and n >= 2:
                            pe.wait_ge(h_done, 2 * DK * f + 2 * n - 2)
                        if f and n and j == 1:
                            turn_back(n - 1)
                        if c == N_CHUNKS - 1:
                            finish_down(c, kb, k0)
                            continue
                        project(pj[:, pair:pair + 2, :], c % 2, kb, lambda xh, k, k0=k0: hid[:, xh, k0 + k, :],
                                start=j == 0, stop=j == 3).then_inc(used, 1)

            def finish_down(c, kb, k0):
                for m in range(2):
                    for k in range(kb):
                        if m == 1 and k == 3:
                            turn_back(len(LAST) - 2)
                        for wh, xh in PRODUCTS:
                            last = nc.tensor.matmul(pj[:, 2 + m, :], w_hl[:, c % 2, wh, k, m * P:(m + 1) * P],
                                                    hid[:, xh, k0 + k, :], start=False,
                                                    stop=k == kb - 1 and (wh, xh) == PRODUCTS[-1])
                    last.then_inc(last_down, 1)

            def mean_square(n):
                pe.wait_ge(acc_done, NPAIR * (n + 1))
                last = nc.tensor.matmul(po[:, 0, :], ones[:, :], scr[:, 0, :], start=True, stop=True)
                if n == 1:
                    for i in range(QT):
                        last = nc.tensor.matmul(po[:, 1, i:i + 1], scr[:, 0, i * P:(i + 1) * P], ones[:, 0:1],
                                                start=True, stop=True)
                last.then_inc(ms_done, 1)

            def turn_back(n):
                at, w = LAST[n]
                pe.wait_ge(h_done, 2 * DK + (at + w) // P)
                if 0 < n < len(LAST) - 1:
                    pe.wait_ge(yt_used, 2 * n)
                    pe.wait_ge(yt_sq, QT * n)
                for i in range(QT):
                    for m in range(w // P):
                        last = nc.tensor.transpose(turned(n, i)[:, m * P:(m + 1) * P],
                                                   h[:, at // P + m, i * P:(i + 1) * P], ident[:, :])
                last.then_inc(yt_done, 1)

            def first_ready(k):
                if k == 0:
                    pe.wait_ge(first_lo, 1)
                elif k == FIRST_KB:
                    pe.wait_ge(lo_done, 1)
                if k in (1, 3):
                    turn_x(k + 3)
                    turn_x(k + 4)
                pe.wait_ge(xn_lo, k + 1)

            ffn_pe(0, 0, first_ready)

            def tile(tau, part=0, parts=1):
                c, m = TILES[tau]
                kind, i, mm = tile_kind(tau)
                slot = (C_MIX + c) % 2
                if part == 0:
                    if m == 0:
                        pe.wait_ge(lo_done, C_MIX + c + 1)
                    for b, before, n in MAY_START[tau]:
                        if before in ROPED:
                            pe.wait_ge(rope_swap, ROPED.index(before) + 1)
                        elif n:
                            pe.wait_ge(tile_read[b], n)
                kb = MIX[c][2]
                if kind == "va":
                    w = w_hl[:, slot, :, :, :].rearrange("p h (k two) n -> p h k (two n)", two=2)
                    for t in BANKS[tau]:
                        for k in range(4):
                            for xh, wh in PRODUCTS:
                                last = nc.tensor.matmul(pj[:, t, :], xn[:, xh, 4 * i + k, t * P:(t + 1) * P],
                                                        w[:, wh, k, :], start=i == 0 and k == 0 and (xh, wh) == (0, 0),
                                                        stop=i == 1 and k == 3 and (xh, wh) == PRODUCTS[-1])
                    last.then_inc(tile_done, 1)
                    return
                bank = bank_of(tau)
                if kind == "vb":
                    for t in range(part * QT // parts, (part + 1) * QT // parts):
                        for k in range(kb):
                            for xh, wh in PRODUCTS:
                                last = nc.tensor.matmul(bank[:, t * P:(t + 1) * P], xn[:, xh, k, t * P:(t + 1) * P],
                                                        w_hl[:, slot, wh, k, P:2 * P],
                                                        start=k == 0 and (xh, wh) == (0, 0),
                                                        stop=k == kb - 1 and (xh, wh) == PRODUCTS[-1])
                    if part == parts - 1:
                        last.then_inc(tile_done, 1)
                    return
                if kind == "ya" and m == 0 and i == 0 and part == 0:
                    pe.wait_ge(o_lo, 4)
                if kind == "yb" and m == 0 and i == 0 and part == 0:
                    pe.wait_ge(o_lo, 8)
                moving = {"ya": lambda xh, k: qa[:, k, xh, :], "yb": lambda xh, k: qb[:, k, xh, :]}.get(kind, of_xn)
                for k in range(part * kb // parts, (part + 1) * kb // parts):
                    for wh, xh in PRODUCTS:
                        last = nc.tensor.matmul(bank, w_hl[:, slot, wh, k, m * P:(m + 1) * P], moving(xh, k),
                                                start=k == 0 and (wh, xh) == (0, 0),
                                                stop=k == kb - 1 and (wh, xh) == PRODUCTS[-1])
                if part == parts - 1:
                    last.then_inc(tile_done, 1)

            def first_tiles():
                pe.wait_ge(lo_done, C_MIX + 1)
                for k in range(DK):
                    if k == DK - 2:
                        mean_square(1)
                    pe.wait_ge(xn_lo, DK + k + 1)
                    for m in range(2):
                        for wh, xh in PRODUCTS:
                            last = nc.tensor.matmul(pj[:, m, :], w_hl[:, C_MIX % 2, wh, k, m * P:(m + 1) * P],
                                                    xn[:, xh, k, :], start=k == 0 and (wh, xh) == (0, 0),
                                                    stop=k == DK - 1 and (wh, xh) == PRODUCTS[-1])
                        if k == DK - 1:
                            last.then_inc(tile_done, 1)

            def wait_tiles(kinds, tile_of=None):
                for tau in range(len(TILES)):
                    kind, i, m = tile_kind(tau)
                    if kind in kinds and not is_partial(tau) and (tile_of is None or tile_of == 2 * i + m):
                        wait_read(pe, tau)

            def scores(s, i):
                b = s >= HEADS
                t, a = (s % HEADS) // 2, s % 2
                q, kt = (qb, 0) if b else (qa, t)
                r = slice(a * HD, (a + 1) * HD)
                if i == 0 and a == 0:
                    wait_tiles(["qb"] if b else ["qa", "ka"], t)
                    if s == HEADS:
                        wait_tiles(["kb"])
                u = QT * s + i
                first, n = n_keys(s, i)
                if u == 1:
                    wait_read(pe, TILES.index((1, 1)))
                if u >= 2:
                    pe.wait_ge(s_used, u - 1)
                for qh, kh in PRODUCTS:
                    last = nc.tensor.matmul(ps[:, u % 2, 0:n], q[r, t, qh, i * P:(i + 1) * P],
                                            kk[r, kt, kh, first:first + n],
                                            start=(qh, kh) == (0, 0), stop=(qh, kh) == PRODUCTS[-1])
                last.then_inc(s_done, 1)

            def transposes(s, i):
                u = QT * s + i
                pe.wait_ge(p_done, u + 1)
                if u >= 2:
                    pe.wait_ge(pt_lo, u - 1)
                to = 0
                for _, nq, c0 in turns(s, i):
                    at = score_at(s, i) + c0
                    last = nc.tensor.transpose(pj[:, 2 + u % 2, to:to + nq], sc[0:nq, s % 2, at:at + P],
                                               ident[0:nq, 0:nq])
                    to += nq
                last.then_inc(t_done, 1)

            def values(s):
                b = s >= HEADS
                pr, a = s // 2, s % 2
                vt = 0 if b else pr
                pe.wait_ge(pt_lo, QT * (s + 1))
                if s == 0:
                    pe.wait_ge(zeros_set, 1)
                if s in (0, HEADS):
                    wait_tiles(["vb"] if b else ["va"])
                if a == 0 and pr >= 2:
                    pe.wait_ge(o_lo, pr - 1)
                for j in range(QT):
                    q1 = min(S, (j + 1) * P + CH) if b else S
                    for vh, ph in PRODUCTS:
                        last = nc.tensor.matmul(po[:, pr % 2, j * P:q1],
                                                vv[:, vt, vh, j, a:a + 2, :], pt[:, ph, j, j * P:q1],
                                                start=a == 0 and j == 0 and (vh, ph) == (0, 0),
                                                stop=a == 1 and j == QT - 1 and (vh, ph) == PRODUCTS[-1],
                                                skip_group_check=True)
                last.then_inc(pv_done, 1)

            first_tiles()
            for tau in range(2, len(BEFORE)):
                tile(tau)
            for i in range(QT):
                scores(0, i)
            tau = len(BEFORE)
            for _tile in FIRST:
                tile(tau)
                tau += 1
            for s in range(NH):
                start = QT - 1 if s in (0, HEADS) else 0
                for i in range(QT):
                    if s + 1 < NH:
                        scores(s + 1, i)
                    if s == 0 and i == 0:
                        wait_read(pe, TILES.index(FIRST[0]))
                    transposes(s, i)
                    if start <= i < QT - 1:
                        tile(tau, i - start, PARTS)
                for part in range(QT - 1 - start, PARTS):
                    tile(tau, part, PARTS)
                tau += 1
                for _tile in FILL[s][1:]:
                    tile(tau)
                    tau += 1
                values(s)
            for _tile in AFTER:
                tile(tau)
                tau += 1

            def merged_ready(k):
                pe.wait_ge(merged_lo, k + 1)

            for n in range(NPAIR):
                c = C_OUT + n
                pair = 2 * (n % 2)
                pe.wait_ge(lo_done, c + 1)
                if n == 0:
                    wait_read(pe, len(TILES) - 4)
                    wait_read(pe, len(TILES) - 3)
                if n >= 2:
                    pe.wait_ge(h_done, DK + 2 * n - 2)
                project(pj[:, pair:pair + 2, :], c % 2, DK,
                        lambda xh, k: pt[:, k // 4, k % 4, :] if xh else qa[:, k // 2, k % 2, :],
                        ready=merged_ready if n == 0 else None).then_inc(used, 1)

            def second_ready(k):
                if k == 0:
                    pe.wait_ge(h_done, DK + 6)
                pe.wait_ge(xn_lo, 2 * DK + k + 1)

            ffn_pe(C_FFN2, 1, second_ready)
            turn_back(len(LAST) - 1)


_INS = ["x", "g_ffn1", "w_ffn1_gu", "w_ffn1_down", "g_mix", "w_in", "a_rel_bias", "b_sinks", "w_branch_a",
        "w_branch_b", "w_out", "g_ffn2", "w_ffn2_gu", "w_ffn2_down", "g_final"]


def kernel(**inputs):
    import numpy as np
    import concourse.bacc as bacc
    from concourse.bass_utils import run_bass_kernel_spmd as run

    half = HD // 2
    freq = np.float32(10000.0) ** (-np.arange(half, dtype=np.float32) / np.float32(half))
    angle = np.arange(S, dtype=np.float32)[None, :] * freq[:, None].astype(np.float32)
    cos, sin = np.cos(angle).astype(np.float32), np.sin(angle).astype(np.float32)
    rope = np.stack([np.concatenate([cos] * 4), np.concatenate([-sin, sin] * 2)], axis=1)

    nc = bacc.Bacc("TRN2", target_bir_lowering=False, num_devices=1)
    arrays, args = {}, []
    named = {name: np.ascontiguousarray(inputs[name]) for name in _INS}
    named["identity"] = np.eye(P, dtype=np.float32)
    named["rope"] = np.ascontiguousarray(rope)
    for name, a in named.items():
        arrays[f"in_{name}"] = a
        args.append(nc.dram_tensor(f"in_{name}", a.shape, mybir.dt.from_np(a.dtype), kind="ExternalInput").ap())
    out = nc.dram_tensor("out_y", (1, S, D), F32, kind="ExternalOutput").ap()
    build(nc, *args, out)
    r = run(nc, [arrays], core_ids=[0])
    return r.results[0]["out_y"]
```
